# Optimizing a Trainium2 kernel written in Bass

```python
import jax, jax.numpy as jnp
from jax import lax
import numpy as np
import math

D_MODEL = 2048
BATCH = 1
SEQ = 256
DEPTH = 1

CHUNK = 64
Q_BLOCK = 128
N_MIXERS = 3
RMS_EPS = 1e-6
SB_HEADS = 16
SB_HEAD_DIM = D_MODEL // SB_HEADS
HG_HEADS = 16
HG_KEY_DIM = D_MODEL // HG_HEADS
HG_VAL_DIM = D_MODEL // HG_HEADS
HG_WIDTH = HG_HEADS * HG_KEY_DIM
MLA_HEADS = 16
MLA_NOPE = 128
MLA_ROPE = 64
MLA_V = 128
MLA_Q_RANK = 768
MLA_KV_RANK = 512
ROPE_THETA = 10000.0
D_FF = 4 * D_MODEL


def _n_layers_of(m):
    return len(range(m, DEPTH, N_MIXERS))

def rms_norm(x, g):
    xf = x.astype(jnp.float32)
    y = xf * lax.rsqrt(jnp.mean(xf * xf, axis=-1, keepdims=True) + RMS_EPS)
    return (y * g.astype(jnp.float32)).astype(x.dtype)

def _sweep_query_blocks(block_fn, queries):
    B, S = queries[0].shape[:2]
    nb = S // Q_BLOCK
    blocked = tuple(a.reshape(B, nb, Q_BLOCK, *a.shape[2:]).swapaxes(0, 1) for a in queries)
    starts = jnp.arange(nb, dtype=jnp.int32) * Q_BLOCK
    out = lax.map(lambda xs: block_fn(xs[0], *xs[1]), (starts, blocked))
    return out.swapaxes(0, 1).reshape(B, S, *out.shape[3:])

def stick_breaking_mixer(h, w_qkv, w_o):
    B, S, _ = h.shape
    qkv = h @ w_qkv
    q, k, v = [a.reshape(B, S, SB_HEADS, SB_HEAD_DIM) for a in jnp.split(qkv, 3, axis=-1)]
    key_idx = jnp.arange(S)
    scale = SB_HEAD_DIM ** -0.5

    def block(q0, qb):
        z = jnp.einsum('bqhd,bkhd->bhqk', qb, k).astype(jnp.float32) * scale
        t = q0 + jnp.arange(Q_BLOCK)
        mask = key_idx[None, :] < t[:, None]
        log_one_minus = jnp.where(mask, -jax.nn.softplus(z), 0.0)
        after = lax.cumsum(log_one_minus, axis=3, reverse=True) - log_one_minus
        A = jnp.where(mask, jnp.exp(jax.nn.log_sigmoid(z) + after), 0.0)
        return jnp.einsum('bhqk,bkhd->bqhd', A.astype(v.dtype), v)

    o = _sweep_query_blocks(block, (q,))
    return o.reshape(B, S, SB_HEADS * SB_HEAD_DIM) @ w_o

def hgrn2_mixer(h, w_in, g_norm, w_o, lb):
    B, S, _ = h.shape
    N = S // CHUNK
    proj = h @ w_in
    q, fz, i, g = jnp.split(proj, [HG_WIDTH, 2 * HG_WIDTH, 2 * HG_WIDTH + HG_HEADS * HG_VAL_DIM], axis=-1)
    fz = fz.astype(jnp.float32)
    log_f = jnp.logaddexp(jnp.log(lb), jnp.log1p(-lb) + jax.nn.log_sigmoid(fz))
    k = (1.0 - lb) * jax.nn.sigmoid(-fz)

    def to_chunks(a, d):
        return a.astype(jnp.float32).reshape(B, N, CHUNK, HG_HEADS, d).transpose(1, 0, 3, 2, 4)

    xs = (to_chunks(q, HG_KEY_DIM), to_chunks(k, HG_KEY_DIM),
          to_chunks(i, HG_VAL_DIM), to_chunks(log_f, HG_KEY_DIM))
    causal = jnp.tril(jnp.ones((CHUNK, CHUNK), dtype=bool))[None, None, :, :, None]

    def step(state, chunk):
        qc, kc, vc, lfc = chunk
        b = jnp.cumsum(lfc, axis=2)
        b_last = b[:, :, -1:, :]
        o_inter = jnp.einsum('bhtc,bhcv->bhtv', qc * jnp.exp(b), state)
        diff = jnp.where(causal, b[:, :, :, None, :] - b[:, :, None, :, :], -jnp.inf)
        scores = jnp.einsum('bhtc,bhsc,bhtsc->bhts', qc, kc, jnp.exp(diff))
        o_intra = jnp.einsum('bhts,bhsv->bhtv', scores, vc)
        new_state = (jnp.exp(b_last[:, :, 0, :])[..., None] * state
                     + jnp.einsum('bhsc,bhsv->bhcv', kc * jnp.exp(b_last - b), vc))
        return new_state, o_inter + o_intra

    state0 = jnp.zeros((B, HG_HEADS, HG_KEY_DIM, HG_VAL_DIM), jnp.float32)
    _, o = lax.scan(step, state0, xs)
    o = o.transpose(1, 0, 3, 2, 4).reshape(B, S, HG_HEADS, HG_VAL_DIM)
    o = o * lax.rsqrt(jnp.mean(o * o, axis=-1, keepdims=True) + RMS_EPS) * g_norm.astype(jnp.float32)
    o = o.reshape(B, S, HG_HEADS * HG_VAL_DIM) * jax.nn.silu(g.astype(jnp.float32))
    return o.astype(h.dtype) @ w_o

def _rope_cos_sin(positions):
    inv_freq = ROPE_THETA ** (-jnp.arange(0, MLA_ROPE, 2, dtype=jnp.float32) / MLA_ROPE)
    ang = positions.astype(jnp.float32)[..., None] * inv_freq
    return jnp.cos(ang), jnp.sin(ang)

def _apply_rope(x, cos, sin):
    x1, x2 = jnp.split(x.astype(jnp.float32), 2, axis=-1)
    return jnp.concatenate([x1 * cos - x2 * sin, x1 * sin + x2 * cos], axis=-1).astype(x.dtype)

def mla_mixer(h, positions, w_dkv, q_norm, kv_norm, w_uq, w_ukv, w_o):
    B, S, _ = h.shape
    c_q, c_kv, k_pe = jnp.split(h @ w_dkv, [MLA_Q_RANK, MLA_Q_RANK + MLA_KV_RANK], axis=-1)
    c_q = rms_norm(c_q, q_norm)
    c_kv = rms_norm(c_kv, kv_norm)
    q = (c_q @ w_uq).reshape(B, S, MLA_HEADS, MLA_NOPE + MLA_ROPE)
    q_nope, q_pe = q[..., :MLA_NOPE], q[..., MLA_NOPE:]
    kv = (c_kv @ w_ukv).reshape(B, S, MLA_HEADS, MLA_NOPE + MLA_V)
    k_nope, v = kv[..., :MLA_NOPE], kv[..., MLA_NOPE:]
    cos, sin = _rope_cos_sin(positions)
    q_pe = _apply_rope(q_pe, cos[:, :, None, :], sin[:, :, None, :])
    k_pe = _apply_rope(k_pe, cos, sin)
    key_chunk = jnp.arange(S) // CHUNK
    scale = (MLA_NOPE + MLA_ROPE) ** -0.5

    def block(q0, qn, qp):
        s = (jnp.einsum('bqhd,bkhd->bhqk', qn, k_nope)
             + jnp.einsum('bqhr,bkr->bhqk', qp, k_pe)).astype(jnp.float32) * scale
        q_chunk = (q0 + jnp.arange(Q_BLOCK)) // CHUNK
        mask = key_chunk[None, :] <= q_chunk[:, None]
        p = jax.nn.softmax(jnp.where(mask, s, -jnp.inf), axis=-1)
        return jnp.einsum('bhqk,bkhd->bqhd', p.astype(v.dtype), v)

    o = _sweep_query_blocks(block, (q_nope, q_pe))
    return o.reshape(B, S, MLA_HEADS * MLA_V) @ w_o

def sq_relu_mlp(h, w1, w2):
    return jnp.square(jax.nn.relu(h @ w1)) @ w2

def first_inputs(seed: int = 0) -> dict:
    key = jax.random.key(seed)
    ks = jax.random.split(key, 20)
    n_sb, n_hg, n_mla = _n_layers_of(0), _n_layers_of(1), _n_layers_of(2)

    def w(k, shape, fan_in):
        return jax.random.normal(k, shape, jnp.float32) * (fan_in ** -0.5)

    def gain(k, shape):
        return 1.0 + 0.02 * jax.random.normal(k, shape, jnp.float32)

    return {
        "x": jax.random.normal(ks[0], (BATCH, SEQ, D_MODEL), jnp.float32),
        "positions": jnp.broadcast_to(jnp.arange(SEQ, dtype=jnp.int32), (BATCH, SEQ)),
        "norm_mix": gain(ks[1], (DEPTH, D_MODEL)),
        "norm_mlp": gain(ks[2], (DEPTH, D_MODEL)),
        "final_norm": gain(ks[3], (D_MODEL,)),
        "sb_w_qkv": w(ks[4], (n_sb, D_MODEL, 3 * SB_HEADS * SB_HEAD_DIM), D_MODEL),
        "sb_w_o": w(ks[5], (n_sb, SB_HEADS * SB_HEAD_DIM, D_MODEL), SB_HEADS * SB_HEAD_DIM),
        "hg_w_in": w(ks[6], (n_hg, D_MODEL, 3 * HG_WIDTH + HG_HEADS * HG_VAL_DIM), D_MODEL),
        "hg_lb_logits": 0.5 * jax.random.normal(ks[7], (DEPTH, HG_WIDTH), jnp.float32),
        "hg_g_norm": gain(ks[8], (n_hg, HG_VAL_DIM)),
        "hg_w_o": w(ks[9], (n_hg, HG_HEADS * HG_VAL_DIM, D_MODEL), HG_HEADS * HG_VAL_DIM),
        "mla_w_dkv": w(ks[10], (n_mla, D_MODEL, MLA_Q_RANK + MLA_KV_RANK + MLA_ROPE), D_MODEL),
        "mla_q_norm": gain(ks[11], (n_mla, MLA_Q_RANK)),
        "mla_kv_norm": gain(ks[12], (n_mla, MLA_KV_RANK)),
        "mla_w_uq": w(ks[13], (n_mla, MLA_Q_RANK, MLA_HEADS * (MLA_NOPE + MLA_ROPE)), MLA_Q_RANK),
        "mla_w_ukv": w(ks[14], (n_mla, MLA_KV_RANK, MLA_HEADS * (MLA_NOPE + MLA_V)), MLA_KV_RANK),
        "mla_w_o": w(ks[15], (n_mla, MLA_HEADS * MLA_V, D_MODEL), MLA_HEADS * MLA_V),
        "mlp_w1": w(ks[16], (DEPTH, D_MODEL, D_FF), D_MODEL),
        "mlp_w2": w(ks[17], (DEPTH, D_FF, D_MODEL), D_FF),
    }

def first_block(x, positions, norm_mix, norm_mlp, final_norm, sb_w_qkv, sb_w_o, hg_w_in,
              hg_lb_logits, hg_g_norm, hg_w_o, mla_w_dkv, mla_q_norm, mla_kv_norm,
              mla_w_uq, mla_w_ukv, mla_w_o, mlp_w1, mlp_w2):
    p_lb = jax.nn.softmax(hg_lb_logits.astype(jnp.float32), axis=0)
    lb_all = jnp.cumsum(p_lb, axis=0) - p_lb[0]
    h = x
    for i in range(DEPTH):
        m, j = i % N_MIXERS, i // N_MIXERS
        a = rms_norm(h, norm_mix[i])
        if m == 0:
            y = stick_breaking_mixer(a, sb_w_qkv[j], sb_w_o[j])
        elif m == 1:
            y = hgrn2_mixer(a, hg_w_in[j], hg_g_norm[j], hg_w_o[j], lb_all[i])
        else:
            y = mla_mixer(a, positions, mla_w_dkv[j], mla_q_norm[j], mla_kv_norm[j],
                          mla_w_uq[j], mla_w_ukv[j], mla_w_o[j])
        h = h + y
        h = h + sq_relu_mlp(rms_norm(h, norm_mlp[i]), mlp_w1[i], mlp_w2[i])
    return rms_norm(h, final_norm)


MIX_WIDTH = D_MODEL
POOL_WIDTH = MIX_WIDTH // 2
POOL_WINDOWS = (2, 4, 8, 16)
POOL_GROUPS = len(POOL_WINDOWS)
POOL_GROUP_DIM = POOL_WIDTH // POOL_GROUPS
NSA_HEADS = 16
NSA_HEAD_DIM = (MIX_WIDTH - POOL_WIDTH) // NSA_HEADS
NSA_KV_GROUPS = 4
NSA_Q_PER_KV = NSA_HEADS // NSA_KV_GROUPS
KV_WIDTH = NSA_KV_GROUPS * NSA_HEAD_DIM
N_BRANCH = 3
CMP_BLOCK = 32
CMP_STRIDE = 16
CMP_HIDDEN = 256
SEL_BLOCK = 64
N_SEL = 8
WINDOW = 512
FORCE_SCORE = 1e4
IN_SPLITS = (POOL_WIDTH, NSA_HEADS * NSA_HEAD_DIM) + (KV_WIDTH,) * 6 + (NSA_HEADS * N_BRANCH,)
IN_WIDTH = sum(IN_SPLITS)
REL_BUCKETS = 32
REL_MAX_DIST = 128
PEER_HEADS = 8
PEER_N_KEYS = 128
PEER_N_EXPERTS = PEER_N_KEYS * PEER_N_KEYS
PEER_QUERY_DIM = 256
PEER_TOPK = 16
PEER_CHUNK = 128
PLE_DIM = 256
NEG_INF = -1e30


def rmsnorm(x, w):
    xf = x.astype(jnp.float32)
    y = xf * lax.rsqrt(jnp.mean(xf * xf, axis=-1, keepdims=True) + RMS_EPS)
    return (y * w.astype(jnp.float32)).astype(x.dtype)

def masked_softmax(logits, mask):
    logits = jnp.where(mask, logits.astype(jnp.float32), NEG_INF)
    m = jnp.max(logits, axis=-1, keepdims=True)
    e = jnp.exp(logits - m) * mask
    return e / jnp.maximum(jnp.sum(e, axis=-1, keepdims=True), 1e-30)

def t5_bucket(rel):
    rel = jnp.maximum(rel, 0)
    exact = REL_BUCKETS // 2
    logr = jnp.log(jnp.maximum(rel, 1).astype(jnp.float32) / exact)
    large = exact + (logr / math.log(REL_MAX_DIST / exact) * (REL_BUCKETS - exact)).astype(jnp.int32)
    return jnp.where(rel < exact, rel, jnp.minimum(large, REL_BUCKETS - 1))

def pool_mixer(u, pool_w, pool_scale):
    B, S, _ = u.shape
    ug = u.reshape(B, S, POOL_GROUPS, POOL_GROUP_DIM).astype(jnp.float32)
    csum = jnp.concatenate([jnp.zeros_like(ug[:, :1]), jnp.cumsum(ug, axis=1)], axis=1)
    t = jnp.arange(S)
    pooled = []
    for g, w in enumerate(POOL_WINDOWS):
        lo = jnp.maximum(t + 1 - w, 0)
        cnt = (t + 1 - lo).astype(jnp.float32)
        cg = csum[:, :, g]
        pooled.append((cg[:, 1:] - cg[:, lo]) / cnt[None, :, None])
    mixed = (jnp.stack(pooled, axis=2) - ug).astype(u.dtype)
    y = jnp.einsum('bsgc,gcd->bsgd', mixed, pool_w).reshape(B, S, POOL_WIDTH)
    return y * pool_scale

def compress(kv, pos, w1, b1, w2):
    B, S, G, dk = kv.shape
    r = CMP_BLOCK // CMP_STRIDE
    nc = S // CMP_STRIDE - r + 1
    seg = kv.reshape(B, S // CMP_STRIDE, CMP_STRIDE, G, dk)
    blocks = jnp.concatenate([seg[:, i:i + nc] for i in range(r)], axis=2)
    blocks = blocks + pos[None, None, :, None, :]
    flat = blocks.transpose(0, 1, 3, 2, 4).reshape(B, nc, G, CMP_BLOCK * dk)
    h = jax.nn.gelu(flat @ w1 + b1, approximate=False)
    return h @ w2

def nsa_attention(q, k_cmp, v_cmp, k_slc, v_slc, k_win, v_win, gates, rel_bias):
    B, S, H, dk = q.shape
    G, R = NSA_KV_GROUPS, NSA_Q_PER_KV
    f32 = jnp.float32
    nc = k_cmp.shape[1]
    nsb = S // SEL_BLOCK
    n_sel = min(N_SEL, nsb)
    q = q.reshape(B, S, G, R, dk)
    gates = gates.reshape(B, S, G, R, N_BRANCH)
    bias_t = rel_bias.T.reshape(G, R, REL_BUCKETS).astype(f32)
    cmp_end = jnp.arange(nc) * CMP_STRIDE + CMP_BLOCK - 1
    c_start = np.arange(nc)[:, None] * CMP_STRIDE
    s_start = np.arange(nsb)[None, :] * SEL_BLOCK
    overlap = np.clip(np.minimum(c_start + CMP_BLOCK, s_start + SEL_BLOCK) - np.maximum(c_start, s_start), 0, None) / CMP_STRIDE
    overlap = jnp.asarray(overlap, f32)
    ks_blk = k_slc.reshape(B, nsb, SEL_BLOCK, G, dk).transpose(0, 3, 1, 2, 4)
    vs_blk = v_slc.reshape(B, nsb, SEL_BLOCK, G, dk).transpose(0, 3, 1, 2, 4)
    kw_pad = jnp.pad(k_win, ((0, 0), (WINDOW, 0), (0, 0), (0, 0)))
    vw_pad = jnp.pad(v_win, ((0, 0), (WINDOW, 0), (0, 0), (0, 0)))
    kc = k_cmp.astype(f32)
    vc = v_cmp.astype(f32)
    b_idx = jnp.arange(B)[:, None, None, None]
    g_idx = jnp.arange(G)[None, :, None, None]
    gi5 = jnp.arange(G)[None, :, None, None, None]
    ri5 = jnp.arange(R)[None, None, :, None, None]
    blk = jnp.arange(nsb)
    scale = dk ** -0.5

    def block_fn(qi):
        q0 = qi * Q_BLOCK
        t = q0 + jnp.arange(Q_BLOCK)
        qf = lax.dynamic_slice_in_dim(q, q0, Q_BLOCK, axis=1).astype(f32) * scale
        gb = lax.dynamic_slice_in_dim(gates, q0, Q_BLOCK, axis=1).astype(f32)
        rel_c = t[:, None] - cmp_end[None, :]
        logit_c = jnp.einsum('bqgrd,bcgd->bgrqc', qf, kc) + bias_t[:, :, t5_bucket(rel_c)]
        p_c = masked_softmax(logit_c, rel_c >= 0)
        o_c = jnp.einsum('bgrqc,bcgd->bqgrd', p_c, vc)
        imp = jnp.einsum('bgqc,cj->bgqj', p_c.sum(axis=2), overlap)
        cur = (t // SEL_BLOCK)[:, None]
        forced = (blk[None, :] == 0) | (blk[None, :] == cur) | (blk[None, :] == cur - 1)
        imp = jnp.where(forced, FORCE_SCORE, jnp.where(blk[None, :] <= cur, imp, NEG_INF))
        _, sel = lax.top_k(imp, n_sel)
        n_k = n_sel * SEL_BLOCK
        ks = ks_blk[b_idx, g_idx, sel].reshape(B, G, Q_BLOCK, n_k, dk).astype(f32)
        vs = vs_blk[b_idx, g_idx, sel].reshape(B, G, Q_BLOCK, n_k, dk).astype(f32)
        pos_s = (sel[..., None] * SEL_BLOCK + jnp.arange(SEL_BLOCK)).reshape(B, G, Q_BLOCK, n_k)
        rel_s = t[None, None, :, None] - pos_s
        bias_s = bias_t[gi5, ri5, t5_bucket(rel_s)[:, :, None]]
        logit_s = jnp.einsum('bqgrd,bgqkd->bgrqk', qf, ks) + bias_s
        p_s = masked_softmax(logit_s, (rel_s >= 0)[:, :, None])
        o_s = jnp.einsum('bgrqk,bgqkd->bqgrd', p_s, vs)
        kw = lax.dynamic_slice_in_dim(kw_pad, q0, WINDOW + Q_BLOCK, axis=1).astype(f32)
        vw = lax.dynamic_slice_in_dim(vw_pad, q0, WINDOW + Q_BLOCK, axis=1).astype(f32)
        pos_w = q0 - WINDOW + jnp.arange(WINDOW + Q_BLOCK)
        rel_w = t[:, None] - pos_w[None, :]
        mask_w = (pos_w[None, :] >= 0) & (rel_w >= 0) & (rel_w < WINDOW)
        logit_w = jnp.einsum('bqgrd,bkgd->bgrqk', qf, kw) + bias_t[:, :, t5_bucket(rel_w)]
        p_w = masked_softmax(logit_w, mask_w)
        o_w = jnp.einsum('bgrqk,bkgd->bqgrd', p_w, vw)
        o = gb[..., 0:1] * o_c + gb[..., 1:2] * o_s + gb[..., 2:3] * o_w
        return o.reshape(B, Q_BLOCK, H * dk).astype(q.dtype)

    out = lax.map(block_fn, jnp.arange(S // Q_BLOCK))
    return out.transpose(1, 0, 2, 3).reshape(B, S, H * dk)

def peer_ffn(xn, w_q, sub_keys, u_tab, v_tab):
    B, S, D = xn.shape
    T = B * S
    xt = xn.reshape(T, D)
    qp = (xt @ w_q).reshape(T, PEER_HEADS, 2, PEER_QUERY_DIM // 2).astype(jnp.float32)
    scores = jnp.einsum('thpd,hpkd->thpk', qp, sub_keys.astype(jnp.float32))
    s_top, i_top = lax.top_k(scores, PEER_TOPK)
    n_cand = PEER_TOPK * PEER_TOPK
    cand_s = (s_top[:, :, 0, :, None] + s_top[:, :, 1, None, :]).reshape(T, PEER_HEADS, n_cand)
    cand_i = (i_top[:, :, 0, :, None] * PEER_N_KEYS + i_top[:, :, 1, None, :]).reshape(T, PEER_HEADS, n_cand)
    best_s, best_pos = lax.top_k(cand_s, PEER_TOPK)
    idx = jnp.take_along_axis(cand_i, best_pos, axis=-1)
    g = jax.nn.softmax(best_s, axis=-1).astype(xn.dtype)
    n_chunks = T // PEER_CHUNK

    def chunk_fn(args):
        xc, ic, gc = args
        h = jax.nn.gelu(jnp.einsum('td,thkd->thk', xc, u_tab[ic]), approximate=False)
        return jnp.einsum('thk,thkd->td', gc * h, v_tab[ic])

    out = lax.map(chunk_fn, (xt.reshape(n_chunks, PEER_CHUNK, D),
                             idx.reshape(n_chunks, PEER_CHUNK, PEER_HEADS, PEER_TOPK),
                             g.reshape(n_chunks, PEER_CHUNK, PEER_HEADS, PEER_TOPK)))
    return out.reshape(B, S, D)

def second_inputs(seed: int = 0) -> dict:
    key = jax.random.key(seed)
    ks = jax.random.split(key, 26)
    f32 = jnp.float32

    def nrm(k, shape, scale):
        return jax.random.normal(k, shape, f32) * scale

    def gain(k, shape):
        return 1.0 + 0.02 * jax.random.normal(k, shape, f32)

    L, D, dk = DEPTH, D_MODEL, NSA_HEAD_DIM
    cmp_in = CMP_BLOCK * dk
    return {
        'x': nrm(ks[0], (BATCH, SEQ, D), 1.0),
        'p': nrm(ks[1], (L, BATCH, SEQ, PLE_DIM), 1.0),
        'rel_bias': nrm(ks[2], (REL_BUCKETS, NSA_HEADS), 0.5),
        'mix_norm_w': gain(ks[3], (L, D)),
        'w_in': nrm(ks[4], (L, D, IN_WIDTH), D ** -0.5),
        'q_norm_w': gain(ks[5], (L, dk)),
        'k_norm_w': gain(ks[6], (L, dk)),
        'cmp_k_pos': nrm(ks[7], (L, CMP_BLOCK, dk), 0.1),
        'cmp_k_w1': nrm(ks[8], (L, cmp_in, CMP_HIDDEN), cmp_in ** -0.5),
        'cmp_k_b1': nrm(ks[9], (L, CMP_HIDDEN), 0.01),
        'cmp_k_w2': nrm(ks[10], (L, CMP_HIDDEN, dk), CMP_HIDDEN ** -0.5),
        'cmp_v_pos': nrm(ks[11], (L, CMP_BLOCK, dk), 0.1),
        'cmp_v_w1': nrm(ks[12], (L, cmp_in, CMP_HIDDEN), cmp_in ** -0.5),
        'cmp_v_b1': nrm(ks[13], (L, CMP_HIDDEN), 0.01),
        'cmp_v_w2': nrm(ks[14], (L, CMP_HIDDEN, dk), CMP_HIDDEN ** -0.5),
        'pool_w': nrm(ks[15], (L, POOL_GROUPS, POOL_GROUP_DIM, POOL_GROUP_DIM), POOL_GROUP_DIM ** -0.5),
        'pool_scale': gain(ks[16], (L, POOL_WIDTH)),
        'w_out': nrm(ks[17], (L, MIX_WIDTH, D), MIX_WIDTH ** -0.5),
        'ffn_norm_w': gain(ks[18], (L, D)),
        'peer_w_q': nrm(ks[19], (L, D, PEER_HEADS * PEER_QUERY_DIM), D ** -0.5),
        'peer_sub_keys': nrm(ks[20], (L, PEER_HEADS, 2, PEER_N_KEYS, PEER_QUERY_DIM // 2), (PEER_QUERY_DIM // 2) ** -0.5),
        'peer_u': nrm(ks[21], (L, PEER_N_EXPERTS, D), D ** -0.5),
        'peer_v': nrm(ks[22], (L, PEER_N_EXPERTS, D), PEER_HEADS ** -0.5),
        'ple_norm_w': gain(ks[23], (L, D)),
        'ple_w_gate': nrm(ks[24], (L, D, D), D ** -0.5),
        'ple_w_proj': nrm(ks[25], (L, PLE_DIM, D), PLE_DIM ** -0.5),
    }

def second_block(x, p, rel_bias, mix_norm_w, w_in, q_norm_w, k_norm_w,
              cmp_k_pos, cmp_k_w1, cmp_k_b1, cmp_k_w2,
              cmp_v_pos, cmp_v_w1, cmp_v_b1, cmp_v_w2,
              pool_w, pool_scale, w_out, ffn_norm_w,
              peer_w_q, peer_sub_keys, peer_u, peer_v,
              ple_norm_w, ple_w_gate, ple_w_proj):
    B, S, _ = x.shape
    H, G, dk = NSA_HEADS, NSA_KV_GROUPS, NSA_HEAD_DIM
    offsets = [int(o) for o in np.cumsum(IN_SPLITS)[:-1]]
    for i in range(DEPTH):
        hn = rmsnorm(x, mix_norm_w[i])
        u, q, kc, vc, ksl, vsl, kwn, vwn, gl = jnp.split(hn @ w_in[i], offsets, axis=-1)
        q = rmsnorm(q.reshape(B, S, H, dk), q_norm_w[i])
        k_cmp = rmsnorm(compress(kc.reshape(B, S, G, dk), cmp_k_pos[i], cmp_k_w1[i], cmp_k_b1[i], cmp_k_w2[i]), k_norm_w[i])
        v_cmp = compress(vc.reshape(B, S, G, dk), cmp_v_pos[i], cmp_v_w1[i], cmp_v_b1[i], cmp_v_w2[i])
        k_slc = rmsnorm(ksl.reshape(B, S, G, dk), k_norm_w[i])
        v_slc = vsl.reshape(B, S, G, dk)
        k_win = rmsnorm(kwn.reshape(B, S, G, dk), k_norm_w[i])
        v_win = vwn.reshape(B, S, G, dk)
        gates = jax.nn.sigmoid(gl.reshape(B, S, H, N_BRANCH))
        attn = nsa_attention(q, k_cmp, v_cmp, k_slc, v_slc, k_win, v_win, gates, rel_bias)
        pool = pool_mixer(u, pool_w[i], pool_scale[i])
        x = x + jnp.concatenate([pool, attn], axis=-1) @ w_out[i]
        x = x + peer_ffn(rmsnorm(x, ffn_norm_w[i]), peer_w_q[i], peer_sub_keys[i], peer_u[i], peer_v[i])
        gate = jax.nn.sigmoid(rmsnorm(x, ple_norm_w[i]) @ ple_w_gate[i])
        x = x + gate * (p[i] @ ple_w_proj[i])
    return x


def setup_inputs(seed=0):
    out = dict(first_inputs(seed))
    for name, value in second_inputs(seed + 1).items():
        if name != "x":
            out[name + "_2"] = value
    return out


def reference(
    x, positions, norm_mix, norm_mlp, final_norm, sb_w_qkv, sb_w_o, hg_w_in, hg_lb_logits,
    hg_g_norm, hg_w_o, mla_w_dkv, mla_q_norm, mla_kv_norm, mla_w_uq, mla_w_ukv, mla_w_o, mlp_w1,
    mlp_w2, p_2, rel_bias_2, mix_norm_w_2, w_in_2, q_norm_w_2, k_norm_w_2, cmp_k_pos_2,
    cmp_k_w1_2, cmp_k_b1_2, cmp_k_w2_2, cmp_v_pos_2, cmp_v_w1_2, cmp_v_b1_2, cmp_v_w2_2,
    pool_w_2, pool_scale_2, w_out_2, ffn_norm_w_2, peer_w_q_2, peer_sub_keys_2, peer_u_2,
    peer_v_2, ple_norm_w_2, ple_w_gate_2, ple_w_proj_2,
):
    x = first_block(
        x, positions, norm_mix, norm_mlp, final_norm, sb_w_qkv, sb_w_o, hg_w_in, hg_lb_logits,
        hg_g_norm, hg_w_o, mla_w_dkv, mla_q_norm, mla_kv_norm, mla_w_uq, mla_w_ukv, mla_w_o,
        mlp_w1, mlp_w2,
    )
    return second_block(
        x, p_2, rel_bias_2, mix_norm_w_2, w_in_2, q_norm_w_2, k_norm_w_2, cmp_k_pos_2,
        cmp_k_w1_2, cmp_k_b1_2, cmp_k_w2_2, cmp_v_pos_2, cmp_v_w1_2, cmp_v_b1_2, cmp_v_w2_2,
        pool_w_2, pool_scale_2, w_out_2, ffn_norm_w_2, peer_w_q_2, peer_sub_keys_2, peer_u_2,
        peer_v_2, ple_norm_w_2, ple_w_gate_2, ple_w_proj_2,
    )


_drawn_inputs = setup_inputs


def setup_inputs(seed=0):
    import zlib

    import numpy as np

    out = dict(_drawn_inputs(seed))
    spreads = {}
    factors = {'mix_norm_w_2': 2.977,
     'q_norm_w_2': 8.0,
     'k_norm_w_2': 8.0,
     'cmp_k_pos_2': 5.661,
     'cmp_k_b1_2': 35.467,
     'cmp_v_b1_2': 64.0,
     'pool_scale_2': 8.637,
     'ffn_norm_w_2': 16.879,
     'ple_norm_w_2': 64.0,
     'rel_bias_2': 2.975,
     'cmp_v_pos_2': 8.0}
    for name, (base, spread) in spreads.items():
        noise = np.random.default_rng([zlib.crc32(name.encode()), seed]).standard_normal(out[name].shape)
        drawn = base * np.exp(spread * noise) if base else spread * noise
        out[name] = __import__('jax').numpy.asarray(drawn.astype(out[name].dtype))
    for name, factor in factors.items():
        out[name] = (out[name] * factor).astype(out[name].dtype)
    return out
```

```python
from contextlib import ExitStack

import numpy as np
import concourse.bass as bass
from concourse import mybir

P = 128
F32 = mybir.dt.float32
U32 = mybir.dt.uint32
ALU = mybir.AluOpType
ACT = mybir.ActivationFunctionType
AX_X = mybir.AxisListType.X

S = 256
D = 2048
MT = S // P
KC = D // P
NT = D // 512
EPS = 1e-6
NEG = -1e30

SB_HEADS = 16
SB_SCALE = (D // SB_HEADS) ** -0.5
SB_GROUPS = 4
TRI_W = 384

D_FF = 8192
G, R, DK = 4, 4, 64
CMP_L, CMP_S, CMP_H = 32, 16, 256
NCMP = S // CMP_S - CMP_L // CMP_S + 1
CPAD = 16
POOL_W = 1024
WIN_REST = 48
PH, NK, TOPK = 8, 128, 16
SLOTS = PH * TOPK
EG = 2
GROUPS = 4

J_QKV, J_WO, J_W1, J_W2, J_WIN = 0, 12, 16, 32, 48
J_CMP, J_MISC, J_WOUT, J_WQ, J_GATE = 56, 57, 58, 62, 66
A_QKV, A_WO, A_W1, A_W2, A_WIN, A_WOUT, A_WQ, A_GATE = 0, 12, 16, 32, 36, 44, 48, 52
_uses = [("gain", 1), ("norm0", 8), ("sb", 48), ("norm1", 8), ("norm2", 8), ("line", 1), ("flip", 12),
         ("qt", 4), ("kt", 2), ("ct", 2), ("mixed", 4), ("pool", 4), ("hid", 2), ("cmp", 1), ("kct", 1),
         ("csc", 2), ("pct", 2), ("att", 64), ("skt", 4), ("norm3", 8), ("psc", 8), ("pt", 1), ("norm4", 8),
         ("pp", 8)]
X = {}
_n = 0
for _name, _count in _uses:
    X[_name] = _n
    _n += _count


def unit_dmas(j, q):
    if j == J_CMP:
        return 2
    if j == J_MISC:
        return (1, 1, 2, 0)[q]
    return 1


def landed(j, q, halves=0):
    return 16 * sum(unit_dmas(i, q) for i in range(j % 2, j + 1, 2)) + 16 * halves


def used(j, halves=0):
    return 8 + 4 * (j + 1) + 8 * halves


def att_use(u, turned):
    return X["att"] + (min(2 * u + 2, 63) if turned else max(2 * u - 1, 0))


def host_constants():
    k, q = np.arange(P)[:, None], np.arange(P)[None, :]
    ident = (k == q).astype(np.float32)
    tri = (k >= q).astype(np.float32)
    ones = np.ones((P, P), np.float32)
    flip = (k + q == P - 1).astype(np.float32)
    strict = np.where(k < q, 0.0, NEG).astype(np.float32)
    neg = np.concatenate([strict, np.zeros((P, P), np.float32), strict], axis=1)
    iota = np.broadcast_to(np.arange(TOPK, dtype=np.float32), (P, TOPK))
    cst = np.concatenate([ident, tri, ones, flip, neg, iota], axis=1)
    band = np.zeros((S, 4, S), np.float32)
    for g, w in enumerate((2, 4, 8, 16)):
        for t in range(S):
            lo = max(t + 1 - w, 0)
            band[lo:t + 1, g, t] = np.float32(1.0) / np.float32(t + 1 - lo)
            band[t, g, t] -= 1.0
    band = np.concatenate([band[:P], band[P:, :, P:]], axis=2)
    onehot = np.zeros((33, 512), np.float32)
    for y in range(511):
        rel = 255 - y
        if rel < 0:
            onehot[32, y] = 1.0
        elif rel < 16:
            onehot[rel, y] = 1.0
        else:
            large = 16 + int(np.float32(np.log(np.float32(rel) / np.float32(16))) / np.float32(np.log(128 / 16)) * np.float32(16))
            onehot[min(large, 31), y] = 1.0
    onehot[32, 511] = 1.0
    return {"cst": np.ascontiguousarray(cst), "band": np.ascontiguousarray(band), "onehot": onehot}


def build(nc, a, out, line_dram):
    with ExitStack() as ctx:
        def sb(name, cols, dt=F32):
            return ctx.enter_context(nc.sbuf_tensor(name, [P, cols], dt))

        def sem(name):
            return ctx.enter_context(nc.semaphore(name))

        ring = sb("ring", 8 * 2048)
        big = sb("big", 16384)
        x_res = sb("x_res", MT * D)
        aT = sb("aT", KC * S)
        oT = sb("oT", KC * S)
        tmp = sb("tmp", MT * D)
        gbc = sb("gbc", D)
        cst = sb("cst", 4 * P + TRI_W + TOPK)
        gT = sb("gT", 80)
        ss = sb("ss", MT * NT)
        ms = sb("ms", MT)
        rt = sb("rt", MT)
        rstd = sb("rstd", MT)
        relb = sb("relb", 16)
        qnw = sb("qnw", DK)
        knw = sb("knw", DK)
        posT = sb("posT", CMP_L)
        b1c = sb("b1c", 4)
        psc = sb("psc", 8)
        gates = sb("gates", MT * WIN_REST)
        nrm = sb("nrm", 3 * 64)
        idx = gbc[:, 0:MT * SLOTS].bitcast(U32)
        gts = gbc[:, MT * SLOTS:2 * MT * SLOTS]
        idxc = sb("idxc", GROUPS * EG, U32)
        hcur = sb("hcur", GROUPS * EG)
        hgel = sb("hgel", GROUPS * EG)
        wcur = sb("wcur", GROUPS * EG)
        banks = [ctx.enter_context(nc.psum_tensor(f"bank{b}", [P, 512], F32)) for b in range(8)]

        ident, tri, ones, flip = (cst[:, n * P:(n + 1) * P] for n in range(4))
        neg = cst[:, 4 * P:4 * P + TRI_W]
        iota16 = cst[:, 4 * P + TRI_W:]

        def v3(t, o, x, y):
            return t[:, o:o + x * y].rearrange("p (x y) -> p x y", x=x)

        slot = [v3(ring, s * 2048, 4, 512) for s in range(8)]
        xr = v3(x_res, 0, MT, D)
        tm = v3(tmp, 0, MT, D)
        aTv = v3(aT, 0, KC, S)
        oTv = v3(oT, 0, KC, S)
        qT, kT, V = v3(big, 0, 4, S), v3(big, 1024, 4, S), v3(big, 2048, MT, 512)
        zm, ee, sp, at = (v3(big, 3072 + n * 1536, 4, TRI_W) for n in range(4))
        hT = v3(big, 0, D_FF // P, S)
        U = v3(big, 0, MT, POOL_W)
        qn = big[:, 2048:4096].rearrange("p (m j r l d) -> p m j r l d", m=MT, j=2, r=R, l=2)
        qn3 = v3(big, 2048, MT * 16, DK)
        qTa = v3(big, 4096, 8, S)
        kvc = v3(big, 6144, MT, 512)
        kn = big[:, 7168:8192].rearrange("p (b m c) -> p b m c", b=2, m=MT)
        kn3 = v3(big, 7168, 16, DK)
        vn = big[:, 8192:9216].rearrange("p (b m c) -> p b m c", b=2, m=MT)
        kTn = big[:, 9216:10240].rearrange("p (b j s) -> p b j s", b=2, j=2)
        TB = v3(big, 10240, 16, TRI_W)
        cT = v3(big, 2048, G, S)
        hc = big[:, 3072:3584].rearrange("p (v h c) -> p v h c", v=2, h=2)
        Vcm = v3(big, 3584, G, DK)
        kcT = big[:, 3840:3968]
        kc2 = v3(big, 3968, 2, DK)
        flat = aT[:, :].rearrange("p (l g c) -> p l g c", l=CMP_L, g=G)
        mixT = v3(gbc, 0, 8, S)
        csc = big[:, 0:512].rearrange("p (l q r j c) -> p l q r j c", l=2, q=MT, r=R, j=2)
        csc3 = v3(big, 0, 32, CPAD)
        cex3 = v3(big, 512, 32, CPAD)
        Pc = big[:, 1024:2048].rearrange("p (q r g c) -> p q r g c", q=MT, r=R, g=G)
        Pc3 = v3(big, 1024, 8, P)
        Xp = [v3(tmp, n * 1536, 4, TRI_W) for n in range(2)]
        sA = [v3(tmp, n * 512, 2, S) for n in range(2)]
        eA = [v3(tmp, 1024 + n * 512, 2, S) for n in range(2)]
        pA = [v3(tmp, 2048 + n * 512, 4, P) for n in range(2)]
        PcT = v3(tmp, 3072, 8, P)
        sk, skT = v3(big, 0, 16, P), v3(big, 2048, 16, P)
        sc, scw = v3(big, 4096, 16, P), v3(big, 6144, 16, P)
        cand, candw = v3(big, 8192, PH, 256), v3(big, 10240, PH, 256)
        oh = v3(big, 12288, SLOTS, TOPK)
        topv = v3(big, 14336, 16, TOPK)
        topi = v3(big, 14592, 16, TOPK).bitcast(U32)
        topf = v3(big, 14848, 16, TOPK)
        bv = v3(big, 15104, PH, TOPK)
        bp = v3(big, 15232, PH, TOPK).bitcast(U32)
        pq = v3(big, 15360, PH, TOPK).bitcast(U32)
        pf = big[:, 15488:15616]
        i1 = big[:, 15616:15744]
        i2 = big[:, 15744:15872]
        bs = big[:, 15872:15904]
        qpT = oTv
        ubuf = [[big[:, (g * 2 + b) * 2048:(g * 2 + b + 1) * 2048] for b in range(EG)] for g in range(GROUPS)]
        vbuf = [[ring[:, (g * 2 + b) * 2048:(g * 2 + b + 1) * 2048] for b in range(EG)] for g in range(GROUPS)]
        xn = tm
        accx = v3(oT, 0, MT, D)
        plew = v3(big, 0, 2, D)
        pin = v3(big, 4096, MT, 256)
        pT = v3(big, 4608, 2, S)
        sg = [[big[:, 5120 + (n * 2 + m) * 512:5120 + (n * 2 + m + 1) * 512] for m in range(MT)] for n in range(2)]

        w_landed = [sem(f"w_landed{s}") for s in range(8)]
        slots_free = sem("slots_free")
        acc_evac = [sem("acc_evac0"), sem("acc_evac1")]
        aux_done = sem("aux_done")
        aux_evac = [sem(f"aux_evac{b}") for b in range(4)]
        cst_landed = sem("cst_landed")
        gain_landed = sem("gain_landed")
        x_landed = sem("x_landed")
        small_landed = sem("small_landed")
        gbc_landed = sem("gbc_landed")
        oh_landed = sem("oh_landed")
        line_stored = sem("line_stored")
        xp_landed = [sem("xp_landed0"), sem("xp_landed1")]
        sk_landed = sem("sk_landed")
        ple_landed = sem("ple_landed")
        sq_done = sem("sq_done")
        ms_ready = sem("ms_ready")
        rt_ready = sem("rt_ready")
        scaled = sem("scaled")
        x2_ready = sem("x2_ready")
        mask_row = sem("mask_row")
        w_done = sem("w_done")
        act_link = sem("act_link")
        dve_link = sem("dve_link")
        soft_ready = sem("soft_ready")
        sp_ready = sem("sp_ready")
        at_ready = sem("at_ready")
        h_ready = sem("h_ready")
        raw_ready = sem("raw_ready")
        qk_norm = sem("qk_norm")
        pads_ready = sem("pads_ready")
        flat_ready = sem("flat_ready")
        head_ms = sem("head_ms")
        head_rt = sem("head_rt")
        kc_ready = sem("kc_ready")
        cmp_shift = sem("cmp_shift")
        cmp_exp = sem("cmp_exp")
        pc_ready = sem("pc_ready")
        s_ready = sem("s_ready")
        e_ready = sem("e_ready")
        p_ready = sem("p_ready")
        pv_done = sem("pv_done")
        pv_evac = sem("pv_evac")
        xn_ready = sem("xn_ready")
        routed = sem("routed")
        best_shift = sem("best_shift")
        best_exp = sem("best_exp")
        idx_ready = sem("idx_ready")
        acc_zero = sem("acc_zero")
        idx_copied = sem("idx_copied")
        u_landed = [sem(f"u_landed{g}") for g in range(GROUPS)]
        v_landed = [sem(f"v_landed{g}") for g in range(GROUPS)]
        dots_done = [sem(f"dots_done{g}") for g in range(GROUPS)]
        gelu_done = [sem(f"gelu_done{g}") for g in range(GROUPS)]
        v_done = [sem(f"v_done{g}") for g in range(GROUPS)]
        peer_added = sem("peer_added")
        gate_exp = sem("gate_exp")
        out_ready = sem("out_ready")
        stored = sem("stored")

        def aux(k):
            return banks[4 + k % 4]

        def wait_aux_free(pe, k, more=0):
            if k >= 4:
                pe.wait_ge(aux_evac[k % 4], k // 4 + more)

        def wait_aux_evac(eng, k, more=0):
            eng.wait_ge(aux_evac[k % 4], k // 4 + 1 + more)

        def wait_acc_evac(eng, n, more=0):
            eng.wait_ge(acc_evac[n % 2], 2 * (n // 2) + 4 + more)

        block = ctx.enter_context(nc.Block())

        @block.sync
        def _(sp):
            def unit(j, q, dst, src, wait, more=0, sems=None):
                if wait:
                    sp.wait_ge(slots_free, 4 * j + q + 1 + more)
                sp.dma_start(dst, src).then_inc(w_landed[4 * (j % 2) + q], 16)

            def job(j, w, n0, k0=0, width=512, more=0):
                rows = w.rearrange("(c p) n -> p c n", p=P)
                for q in range(4):
                    unit(j, q, slot[4 * (j % 2) + q][:, :, 0:width],
                         rows[:, k0 + 4 * q:k0 + 4 * q + 4, bass.ds(n0, width)], True, more)

            sp.dma_start(xr, a["x"].rearrange("(m p) d -> p m d", p=P)).then_inc(x_landed, 16)
            with sp.Fori(0, 2) as i:
                for g in range(2):
                    for w in range(3):
                        job(J_QKV + 3 * g + w, a["sb_w_qkv"], i * 1024 + w * D + g * 512, more=i * 24)
            with sp.Fori(0, 2) as i:
                for n in range(2):
                    job(J_WO + n, a["sb_w_o"], i * 1024 + n * 512, more=i * 8)
            with sp.Fori(0, 8) as i:
                for n in range(2):
                    job(J_W1 + n, a["mlp_w1"], i * 1024 + n * 512, more=i * 8)
            with sp.Fori(0, 2) as i:
                for n in range(2):
                    for kq in range(4):
                        job(J_W2 + 4 * n + kq, a["mlp_w2"], i * 1024 + n * 512, k0=16 * kq, more=i * 32)
            for n in range(8):
                job(J_WIN + n, a["w_in"], n * 512, width=512 if n < 7 else WIN_REST)
                if n == 0:
                    sp.wait_ge(x2_ready, 2)
                    sp.dma_start(gbc[0:33, 512:1024], a["onehot"]).then_inc(oh_landed, 16)
                if n == 2:
                    wait_aux_evac(sp, X["line"])
                    sp.dma_start(line_dram, gbc[0:16, 0:512]).then_inc(line_stored, 16)
                    sp.wait_ge(line_stored, 16)
                    for n4 in range(2):
                        sp.dma_start(Xp[n4], bass.AP(line_dram.tensor, n4 * 4 * 512, [[1, P], [512, 4], [1, TRI_W]])
                                     ).then_inc(xp_landed[n4], 16)
                if n == 4:
                    for n4 in range(2, 4):
                        wait_aux_evac(sp, X["flip"] + 3 * (n4 - 2) + 2)
                        sp.dma_start(Xp[n4 - 2], bass.AP(line_dram.tensor, n4 * 4 * 512, [[1, P], [512, 4], [1, TRI_W]])
                                     ).then_inc(xp_landed[n4 - 2], 16)
            for q in range(4):
                for v, name in enumerate(("cmp_k_w1", "cmp_v_w1")):
                    rows = a[name].rearrange("(l d) n -> d l n", d=DK)
                    unit(J_CMP, q, v3(ring, q * 2048, 8, CMP_H)[v * DK:(v + 1) * DK],
                         rows[:, 8 * q:8 * q + 8, :], v == 0)
            unit(J_MISC, 0, v3(ring, 4 * 2048, 8, 256), a["pool_w"].rearrange("g (c p) d -> p (g c) d", p=P), True)
            unit(J_MISC, 1, ring[:, 5 * 2048:5 * 2048 + 4 * TRI_W], a["band"].rearrange("p g t -> p (g t)"), True)
            for v, name in enumerate(("cmp_k_w2", "cmp_v_w2")):
                unit(J_MISC, 2, v3(ring, 6 * 2048 + v * P, 2, DK), a[name].rearrange("(h p) d -> p h d", p=P), v == 0)
            for base, w in ((J_WOUT, a["w_out"]), (J_WQ, a["peer_w_q"])):
                with sp.Fori(0, 2) as i:
                    for n in range(2):
                        job(base + n, w, i * 1024 + n * 512, more=i * 8)
                if base == J_WOUT:
                    sp.dma_start(sk, a["peer_sub_keys"].rearrange("h b k d -> k (h b) d")).then_inc(sk_landed, 16)
            for g in range(GROUPS):
                sp.wait_ge(v_done[g], MT * SLOTS // (GROUPS * EG) * EG + EG)
            for n in range(2):
                job(J_GATE + n, a["ple_w_gate"], n * 512)
            sp.dma_start(plew, a["ple_w_proj"].rearrange("(c p) n -> p c n", p=P)).then_inc(ple_landed, 16)
            sp.dma_start(pin, a["p"].rearrange("(m p) d -> p m d", p=P)).then_inc(ple_landed, 16)
            for n in range(2, 4):
                job(J_GATE + n, a["ple_w_gate"], n * 512)
            for n in range(NT):
                sp.wait_ge(out_ready, 2 * (n + 1))
                sp.dma_start(out.rearrange("(m p) d -> p m d", p=P)[:, :, n * 512:(n + 1) * 512],
                             xr[:, :, n * 512:(n + 1) * 512]).then_inc(stored, 16)
            sp.wait_ge(stored, 16 * NT)

        @block.scalar
        def _(act):
            links = [0]

            def link(ins):
                links[0] += 1
                ins.then_inc(act_link, 1)
                act.wait_ge(act_link, links[0])

            act.dma_start(cst[:, :], a["cst"]).then_inc(cst_landed, 16)
            for n, name in enumerate(("norm_mix", "norm_mlp", "mix_norm_w", "ffn_norm_w", "ple_norm_w")):
                act.dma_start(tmp[16 * n:16 * n + 16, 0:P], a[name].rearrange("(c p) -> c p", p=P)
                              ).then_inc(gain_landed, 16)
            act.dma_start(gbc[:, :], a["final_norm"].rearrange("(o d) -> o d", o=1).broadcast_to((P, D))
                          ).then_inc(gbc_landed, 16)
            with nc.allow_non_contiguous_dma(reason="small tables"):
                act.dma_start(relb[0:32, :], a["rel_bias"]).then_inc(small_landed, 16)
                act.dma_start(qnw[:, :], a["q_norm_w"].rearrange("(o d) -> o d", o=1).broadcast_to((P, DK))
                              ).then_inc(small_landed, 16)
                act.dma_start(knw[:, :], a["k_norm_w"].rearrange("(o d) -> o d", o=1).broadcast_to((P, DK))
                              ).then_inc(small_landed, 16)
                for v, name in enumerate(("cmp_k", "cmp_v")):
                    act.dma_start(posT[v * DK:(v + 1) * DK, :], a[name + "_pos"].rearrange("l d -> d l")
                                  ).then_inc(small_landed, 16)
                    act.dma_start(b1c[:, 2 * v:2 * v + 2], a[name + "_b1"].rearrange("(h p) -> p h", p=P)
                                  ).then_inc(small_landed, 16)
                act.dma_start(psc[:, :], a["pool_scale"].rearrange("(c p) -> p c", p=P)).then_inc(small_landed, 16)

            def squares(cols, piece):
                for m in range(MT):
                    nc.scalar.activation(tm[:, m, cols], xr[:, m, cols], ACT.Square,
                                         accum_out=ss[:, piece(m)]).then_inc(sq_done, 1)

            def all_squares():
                for n in range(NT):
                    squares(slice(n * 512, n * 512 + 512), lambda m: slice(m * NT + n, m * NT + n + 1))

            def root(n):
                act.wait_ge(ms_ready, n + 1)
                nc.scalar.activation(rt[:, :], ms[:, :], ACT.Sqrt).then_inc(rt_ready, 1)

            def residual_squares(a0, pairs):
                with act.Fori(0, pairs) as i:
                    for n in range(2):
                        wait_acc_evac(act, a0 + n, i * 2)
                        squares(bass.ds(i * 1024 + n * 512, 512), lambda m: bass.ds(i * 2 + (m * NT + n), 1))

            act.wait_ge(x_landed, 16)
            wait_aux_evac(act, X["gain"])
            all_squares()
            root(0)

            with act.Fori(0, 2) as i:
                for g in range(2):
                    ka = A_QKV + 3 * g + 1
                    act.wait_ge(slots_free, used(J_QKV + 3 * g + 1, i * 3))
                    for b in range(2):
                        nc.scalar.copy(kT[:, 2 * b:2 * b + 2, :], banks[2 * (ka % 2) + b][:, :].rearrange(
                            "p (h s) -> p h s", h=2)).then_inc(acc_evac[ka % 2], 1)
                    wait_aux_evac(act, X["sb"] + 12 * g + 3, i * 6)
                    n0 = 3 * g
                    nc.scalar.activation(ee, zm, ACT.Abs).then_inc(soft_ready, 1)
                    act.wait_ge(soft_ready, n0 + 1 + i * 6)
                    nc.scalar.activation(ee, ee, ACT.Exp, scale=-1.0).then_inc(soft_ready, 1)
                    act.wait_ge(soft_ready, n0 + 2 + i * 6)
                    nc.scalar.activation(ee, ee, ACT.Ln, bias=1.0).then_inc(soft_ready, 1)
                    va = A_QKV + 3 * g + 2
                    act.wait_ge(slots_free, used(J_QKV + 3 * g + 2, i * 3))
                    for m in range(MT):
                        nc.scalar.copy(V[:, m, :], banks[2 * (va % 2) + m][:, :]).then_inc(acc_evac[va % 2], 1)
                    wait_aux_evac(act, X["sb"] + 12 * g + 7, i * 6)
                    nc.scalar.activation(at, at, ACT.Exp).then_inc(at_ready, 1)
            residual_squares(A_WO, 2)
            root(1)

            with act.Fori(0, 8) as i:
                for n in range(2):
                    act.wait_ge(slots_free, used(J_W1 + n, i))
                    for b in range(2):
                        nc.scalar.activation(big[:, bass.ds(i * 2048 + (n * 1024 + b * 512), 512)],
                                             banks[2 * n + b][:, :], ACT.Relu).then_inc(acc_evac[n], 1)
            residual_squares(A_W2, 2)
            root(2)
            act.wait_ge(x2_ready, 2)
            all_squares()
            root(3)

            def win(n):
                act.wait_ge(slots_free, used(J_WIN + n))
                return [banks[2 * (n % 2) + m] for m in range(MT)]

            for n in range(8):
                ps = win(n)
                for m in range(MT):
                    if n < 2:
                        nc.scalar.copy(U[:, m, n * 512:n * 512 + 512], ps[m][:, :]).then_inc(acc_evac[n % 2], 1)
                    elif n < 4:
                        for l in range(2):
                            q_raw = nc.scalar.copy(qn[:, m, n - 2, :, l, :], ps[m][:, l * 256:l * 256 + 256].rearrange(
                                "p (r d) -> p r d", r=R))
                        q_raw.then_inc(acc_evac[n % 2], 1)
                    elif n == 4:
                        nc.scalar.copy(kvc[:, m, :].rearrange("p (g v d) -> p v g d", g=G, v=2),
                                       ps[m][:, :].rearrange("p (v g d) -> p v g d", v=2, g=G)).then_inc(acc_evac[n % 2], 1)
                    elif n < 7:
                        nc.scalar.copy(kn[:, n - 5, m, :], ps[m][:, 0:256])
                        nc.scalar.copy(vn[:, n - 5, m, :], ps[m][:, 256:512]).then_inc(acc_evac[n % 2], 1)
                    else:
                        nc.scalar.activation(gates[:, m * WIN_REST:(m + 1) * WIN_REST], ps[m][:, 0:WIN_REST],
                                             ACT.Sigmoid).then_inc(acc_evac[n % 2], 1)
            act.wait_ge(head_ms, 1)
            nc.scalar.activation(nrm[:, 64:96], nrm[:, 0:32], ACT.Sqrt).then_inc(head_rt, 1)
            act.wait_ge(head_ms, 2)
            nc.scalar.activation(nrm[:, 96:112], nrm[:, 32:48], ACT.Sqrt).then_inc(head_rt, 1)
            act.wait_ge(small_landed, 16 * 8)
            for v in range(2):
                k = X["hid"] + v
                act.wait_ge(aux_done, k + 1)
                for h in range(2):
                    g1 = nc.scalar.activation(hc[:, v, h, :], aux(k)[:, h * P:h * P + P], ACT.Gelu,
                                              bias=b1c[:, 2 * v + h:2 * v + h + 1])
                g1.then_inc(aux_evac[k % 4], 1)
            act.wait_ge(head_ms, 3)
            nc.scalar.activation(nrm[:, 112:113], nrm[:, 48:49], ACT.Sqrt).then_inc(head_rt, 1)
            act.wait_ge(cmp_shift, 1)
            nc.scalar.activation(cex3, csc3, ACT.Exp).then_inc(cmp_exp, 1)
            for u in range(32):
                w = P * (u % 2 + 1)
                act.wait_ge(s_ready, u + 1)
                for b in range(2):
                    e = nc.scalar.activation(eA[u % 2][:, b, 0:w], sA[u % 2][:, b, 0:w], ACT.Exp,
                                             bias=nrm[:, 4 * (u % 2) + b:4 * (u % 2) + b + 1],
                                             accum_out=nrm[:, 4 * (u % 2) + 2 + b:4 * (u % 2) + 3 + b])
                    e.then_inc(e_ready, 1)
            act.wait_ge(pv_evac, 8)
            act.dma_start(gbc[:, :], a["ffn_norm_w"].rearrange("(o d) -> o d", o=1).broadcast_to((P, D))
                          ).then_inc(gbc_landed, 16)
            residual_squares(A_WOUT, 2)
            root(4)

            with act.Fori(0, 2) as i:
                for n in range(2):
                    act.wait_ge(slots_free, used(J_WQ + n, i))
                    for b in range(2):
                        nc.scalar.copy(oT[:, bass.ds(i * 2048 + (n * 1024 + b * 512), 512)],
                                       banks[2 * n + b][:, :]).then_inc(acc_evac[n], 1)
            for m in range(MT):
                if m:
                    act.wait_ge(routed, m)
                for n in range(4):
                    k = X["psc"] + 4 * m + n
                    act.wait_ge(aux_done, k + 1)
                    nc.scalar.copy(sc[:, 4 * n:4 * n + 4, :], aux(k)[:, :].rearrange("p (h k) -> p h k", h=4)
                                   ).then_inc(aux_evac[k % 4], 1)
                act.wait_ge(best_shift, m + 1)
                nc.scalar.activation(bv, bv, ACT.Exp).then_inc(best_exp, 1)
            for m in range(MT):
                per = SLOTS // (GROUPS * EG)
                with act.Fori(0, per) as i:
                    for g in range(GROUPS):
                        act.wait_ge(dots_done[g], EG * (m * per + 1) + i * EG)
                        nc.scalar.activation(hgel[:, g * EG:(g + 1) * EG], hcur[:, g * EG:(g + 1) * EG], ACT.Gelu
                                             ).then_inc(gelu_done[g], 1)
            act.wait_ge(peer_added, MT)
            all_squares()
            root(5)
            for n in range(NT):
                act.wait_ge(slots_free, used(J_GATE + n))
                if n >= 2:
                    act.wait_ge(out_ready, 2 * (n - 1))
                for m in range(MT):
                    nc.scalar.activation(sg[n % 2][m], banks[2 * (n % 2) + m][:, :], ACT.Sigmoid
                                         ).then_inc(acc_evac[n % 2], 1)

        @block.vector
        def _(dve):
            links = [0]

            def link(ins):
                links[0] += 1
                ins.then_inc(dve_link, 1)
                dve.wait_ge(dve_link, links[0])

            V_ = nc.vector

            def rms(n):
                dve.wait_ge(sq_done, 8 * (n + 1))
                link(V_.tensor_reduce(ms[:, :], v3(ss, 0, MT, NT), AX_X, ALU.add))
                V_.tensor_scalar(ms[:, :], ms[:, :], 1.0 / D, EPS, ALU.mult, ALU.add).then_inc(ms_ready, 1)
                dve.wait_ge(rt_ready, n + 1)
                link(V_.reciprocal(rstd[:, :], rt[:, :]))

            def scale_rows():
                for m in range(MT):
                    V_.tensor_scalar(tm[:, m, :], xr[:, m, :], rstd[:, m:m + 1], None, ALU.mult).then_inc(scaled, 1)

            def take_transposed(k0, gain):
                for u in range(8):
                    k = k0 + u
                    dve.wait_ge(aux_done, k + 1)
                    V_.tensor_tensor(aTv[:, 2 * u:2 * u + 2, :], aux(k)[:, :].rearrange("p (c s) -> p c s", c=2),
                                     gT[:, 16 * gain + 2 * u:16 * gain + 2 * u + 2].unsqueeze(2).broadcast_to((P, 2, S)),
                                     ALU.mult).then_inc(aux_evac[k % 4], 1)

            def residual(j0, jn, pairs):
                with dve.Fori(0, pairs) as i:
                    for n in range(2):
                        dve.wait_ge(slots_free, used(j0 + jn * n, i * jn))
                        for m in range(MT):
                            cols = bass.ds(i * 1024 + n * 512, 512)
                            V_.tensor_tensor(xr[:, m, cols], xr[:, m, cols], banks[2 * n + m][:, :], ALU.add
                                             ).then_inc(acc_evac[n], 1)

            V_.memset(relb[32:33, :], NEG).then_inc(mask_row, 1)
            dve.wait_ge(aux_done, X["gain"] + 1)
            V_.tensor_copy(gT[:, :], aux(X["gain"])[:, 0:80]).then_inc(aux_evac[X["gain"] % 4], 1)
            rms(0)
            scale_rows()
            take_transposed(X["norm0"], 0)

            with dve.Fori(0, 2) as i:
                for g in range(2):
                    ps = 3 * g % 2
                    dve.wait_ge(slots_free, used(J_QKV + 3 * g, i * 3))
                    for b in range(2):
                        V_.tensor_scalar(qT[:, 2 * b:2 * b + 2, :], banks[2 * ps + b][:, :].rearrange(
                            "p (h s) -> p h s", h=2), SB_SCALE, None, ALU.mult).then_inc(acc_evac[ps], 1)
                    if g == 1:
                        for h in range(4):
                            k = X["sb"] + 8 + h
                            dve.wait_ge(aux_done, k + 1 + i * 24)
                            V_.tensor_copy(oT[:, bass.ds(i * 2048 + h * S, S)], aux(k)[:, 0:S]
                                           ).then_inc(aux_evac[k % 4], 1)
                    for h in range(4):
                        k = X["sb"] + 12 * g + h
                        dve.wait_ge(aux_done, k + 1 + i * 24)
                        V_.tensor_tensor(zm[:, h, :], aux(k)[:, 0:TRI_W], neg, ALU.add).then_inc(aux_evac[k % 4], 1)
                    dve.wait_ge(soft_ready, 3 * g + 3 + i * 6)
                    V_.scalar_tensor_tensor(sp, zm, 0.0, ee, ALU.max, ALU.add).then_inc(sp_ready, 1)
                    for h in range(4):
                        k = X["sb"] + 12 * g + 4 + h
                        dve.wait_ge(aux_done, k + 1 + i * 24)
                        V_.tensor_tensor(at[:, h, :], zm[:, h, :], aux(k)[:, 0:TRI_W], ALU.subtract
                                         ).then_inc(aux_evac[k % 4], 1)
                for h in range(4):
                    k = X["sb"] + 20 + h
                    dve.wait_ge(aux_done, k + 1 + i * 24)
                    V_.tensor_copy(oT[:, bass.ds(i * 2048 + (1024 + h * S), S)], aux(k)[:, 0:S]
                                   ).then_inc(aux_evac[k % 4], 1)
            residual(J_WO, 1, 2)
            rms(1)
            scale_rows()
            take_transposed(X["norm1"], 1)

            with dve.Fori(0, 8) as i:
                for n in range(2):
                    wait_acc_evac(dve, A_W1 + n, i * 2)
                    for b in range(2):
                        h = big[:, bass.ds(i * 2048 + (n * 1024 + b * 512), 512)]
                        V_.tensor_tensor(h, h, h, ALU.mult).then_inc(h_ready, 1)
            residual(J_W2 + 3, 4, 2)
            rms(2)
            dve.wait_ge(gbc_landed, 16)
            for m in range(MT):
                V_.scalar_tensor_tensor(xr[:, m, :], xr[:, m, :], rstd[:, m:m + 1], gbc[:, :], ALU.mult, ALU.mult
                                        ).then_inc(x2_ready, 1)
            rms(3)
            dve.wait_ge(x2_ready, 2)
            scale_rows()
            take_transposed(X["norm2"], 2)

            dve.wait_ge(aux_done, X["line"] + 1)
            V_.tensor_copy(gbc[0:16, 0:512], aux(X["line"])[0:16, :]).then_inc(aux_evac[X["line"] % 4], 1)
            for f in range(12):
                k = X["flip"] + f
                dve.wait_ge(aux_done, k + 1)
                V_.tensor_copy(big[:, 10240 + f * 512:10240 + f * 512 + 512], aux(k)[:, :]
                               ).then_inc(aux_evac[k % 4], 1)

            def head_norm(t3, heads, at_, sq, n):
                link(V_.tensor_tensor(sq, t3, t3, ALU.mult))
                link(V_.tensor_reduce(nrm[:, at_:at_ + heads], sq, AX_X, ALU.add))
                V_.tensor_scalar(nrm[:, at_:at_ + heads], nrm[:, at_:at_ + heads], 1.0 / DK, EPS, ALU.mult, ALU.add
                                 ).then_inc(head_ms, 1)
                dve.wait_ge(head_rt, n + 1)
                link(V_.reciprocal(nrm[:, at_ + 128:at_ + 128 + heads], nrm[:, at_ + 64:at_ + 64 + heads]))
                return nrm[:, at_ + 128:at_ + 128 + heads].unsqueeze(2)

            wait_acc_evac(dve, A_WIN + 3)
            wait_acc_evac(dve, A_WIN + 2)
            r = head_norm(qn3, 32, 0, v3(tmp, 0, 32, DK), 0)
            link(V_.tensor_tensor(qn3, qn3, r.broadcast_to((P, 32, DK)), ALU.mult))
            V_.scalar_tensor_tensor(qn3, qn3, DK ** -0.5, qnw[:, :].unsqueeze(1).broadcast_to((P, 32, DK)),
                                    ALU.mult, ALU.mult).then_inc(qk_norm, 1)
            wait_acc_evac(dve, A_WIN + 5)
            wait_acc_evac(dve, A_WIN + 6)
            r = head_norm(kn3, 16, 32, v3(tmp, 2048, 16, DK), 1)
            link(V_.tensor_tensor(kn3, kn3, r.broadcast_to((P, 16, DK)), ALU.mult))
            V_.tensor_tensor(kn3, kn3, knw[:, :].unsqueeze(1).broadcast_to((P, 16, DK)), ALU.mult
                             ).then_inc(qk_norm, 1)
            wait_acc_evac(dve, A_WIN + 7)
            for k0, n, dst in ((X["qt"], 4, 4096), (X["kt"], 2, 9216)):
                for u in range(n):
                    k = k0 + u
                    dve.wait_ge(aux_done, k + 1)
                    V_.tensor_copy(big[:, dst + u * 512:dst + u * 512 + 512], aux(k)[:, :]).then_inc(aux_evac[k % 4], 1)
            for u in range(2):
                k = X["ct"] + u
                dve.wait_ge(aux_done, k + 1)
                V_.tensor_copy(cT[:, 2 * u:2 * u + 2, :], aux(k)[:, :].rearrange("p (g s) -> p g s", g=2)
                               ).then_inc(aux_evac[k % 4], 1)
            wait_aux_evac(dve, X["ct"] + 1)
            dve.wait_ge(slots_free, used(J_WIN + 7))
            for g in range(G):
                for half in range(2):
                    src = cT[:, g, 16 * half:16 * half + 16 * NCMP].rearrange("p (c l) -> p c l", l=16)
                    last = V_.tensor_tensor(flat[:, 16 * half:16 * half + 16, g, 0:NCMP].rearrange("p l c -> p c l"), src,
                                            posT[:, 16 * half:16 * half + 16].unsqueeze(1).broadcast_to((P, NCMP, 16)),
                                            ALU.add)
            last.then_inc(flat_ready, 1)
            for u in range(4):
                k = X["mixed"] + u
                dve.wait_ge(aux_done, k + 1)
                V_.tensor_copy(mixT[:, 2 * u:2 * u + 2, :], aux(k)[:, :].rearrange("p (c s) -> p c s", c=2)
                               ).then_inc(aux_evac[k % 4], 1)
            for g in range(4):
                k = X["pool"] + g
                dve.wait_ge(aux_done, k + 1)
                V_.tensor_tensor(oTv[:, 2 * g:2 * g + 2, :], aux(k)[:, :].rearrange("p (c s) -> p c s", c=2),
                                 psc[:, 2 * g:2 * g + 2].unsqueeze(2).broadcast_to((P, 2, S)), ALU.mult
                                 ).then_inc(aux_evac[k % 4], 1)
            k = X["cmp"]
            dve.wait_ge(pads_ready, 2)
            dve.wait_ge(aux_done, k + 1)
            for g in range(G):
                V_.tensor_copy(Vcm[32 * g:32 * g + NCMP, g, :], aux(k)[32 * g:32 * g + NCMP, DK:2 * DK])
            link(V_.tensor_copy(kc2[:, 0, :], aux(k)[:, 0:DK]))
            link(V_.tensor_tensor(kc2[:, 1, :], kc2[:, 0, :], kc2[:, 0, :], ALU.mult))
            link(V_.tensor_reduce(nrm[:, 48:49], kc2[:, 1, :], AX_X, ALU.add))
            V_.tensor_scalar(nrm[:, 48:49], nrm[:, 48:49], 1.0 / DK, EPS, ALU.mult, ALU.add).then_inc(head_ms, 1)
            dve.wait_ge(head_rt, 3)
            link(V_.reciprocal(nrm[:, 176:177], nrm[:, 112:113]))
            link(V_.scalar_tensor_tensor(kc2[:, 0, :], kc2[:, 0, :], nrm[:, 176:177], knw[:, :], ALU.mult, ALU.mult))
            V_.tensor_copy(kc2[:, 1, :], kc2[:, 0, :]).then_inc(aux_evac[k % 4], 1)
            k = X["kct"]
            dve.wait_ge(aux_done, k + 1)
            V_.tensor_copy(kcT, aux(k)[:, 0:P]).then_inc(aux_evac[k % 4], 1)
            V_.memset(csc3[:, :, NCMP:CPAD], NEG)
            for l in range(2):
                k = X["csc"] + l
                dve.wait_ge(aux_done, k + 1)
                for q in range(MT):
                    off = 255 - P * q - (P - 1) + CMP_L - 1
                    for j in range(2):
                        bias = TB[:, (2 * j + l) * R:(2 * j + l) * R + R, off:off + CMP_S * (NCMP - 1) + 1:CMP_S]
                        pv = aux(k)[:, q * P:(q + 1) * P].rearrange("p (r j c) -> p r j c", r=R, j=2)
                        last = V_.tensor_tensor(csc[:, l, q, :, j, 0:NCMP], pv[:, :, j, 0:NCMP], bias, ALU.add)
                last.then_inc(aux_evac[k % 4], 1)
            wait_aux_evac(dve, X["csc"] + 1)
            link(V_.tensor_reduce(nrm[:, 0:32], csc3, AX_X, ALU.max))
            link(V_.tensor_scalar(Pc3[:, 0:4, :].rearrange("p a (b c) -> p (a b) c", c=CPAD), csc3, NEG / 2, None,
                                  ALU.is_gt))
            V_.tensor_tensor(csc3, csc3, nrm[:, 0:32].unsqueeze(2).broadcast_to((P, 32, CPAD)), ALU.subtract
                             ).then_inc(cmp_shift, 1)
            dve.wait_ge(cmp_exp, 1)
            mask = Pc3[:, 0:4, :].rearrange("p a (b c) -> p (a b) c", c=CPAD)
            link(V_.tensor_tensor(cex3, cex3, mask, ALU.mult))
            link(V_.tensor_reduce(nrm[:, 32:64], cex3, AX_X, ALU.add))
            link(V_.tensor_scalar(nrm[:, 32:64], nrm[:, 32:64], 1e-30, None, ALU.max))
            link(V_.reciprocal(nrm[:, 64:96], nrm[:, 32:64]))
            rc = nrm[:, 64:96].rearrange("p (l q r j) -> p l q r j", l=2, q=MT, r=R)
            gv = gates[:, :].rearrange("p (m j l r b) -> p m j l r b", m=MT, j=2, l=2, r=R)
            for l in range(2):
                for q in range(MT):
                    last = V_.tensor_tensor(rc[:, l, q, :, :].rearrange("p r j -> p j r"),
                                            rc[:, l, q, :, :].rearrange("p r j -> p j r"),
                                            gv[:, q, :, l, :, 0], ALU.mult)
            link(last)
            link(V_.memset(big[:, 1024:2048], 0.0))
            cexv = cex3[:, :, :].rearrange("p (l q r j) c -> p l q r j c", l=2, q=MT, r=R)
            for l in range(2):
                for q in range(MT):
                    for j in range(2):
                        last = V_.tensor_tensor(Pc[:, q, :, 2 * j + l, 0:CPAD], cexv[:, l, q, :, j, :],
                                                rc[:, l, q, :, j].unsqueeze(2).broadcast_to((P, R, CPAD)), ALU.mult)
            last.then_inc(pc_ready, 1)
            for u in range(2):
                k = X["pct"] + u
                dve.wait_ge(aux_done, k + 1)
                V_.tensor_copy(PcT[:, 4 * u:4 * u + 4, :], aux(k)[:, :].rearrange("p (n s) -> p n s", n=4)
                               ).then_inc(aux_evac[k % 4], 1)

            def logits(u):
                h, q = u // 2, u % 2
                w = P * (q + 1)
                k = att_use(u, 0)
                dve.wait_ge(aux_done, k + 1)
                if u >= 2:
                    dve.wait_ge(e_ready, 2 * (u - 1))
                (V_.tensor_tensor(sA[q][:, :, 0:w], aux(k)[:, :].rearrange(
                    "p (b s) -> p b s", b=2)[:, :, 0:w], TB[:, h, S - w:S].unsqueeze(1).broadcast_to((P, 2, w)), ALU.add)
                 ).then_inc(aux_evac[k % 4], 1)
                wait_aux_evac(dve, k)
                link(V_.tensor_reduce(nrm[:, 4 * q:4 * q + 2], sA[q][:, :, 0:w], AX_X, ALU.max))
                V_.tensor_scalar(nrm[:, 4 * q:4 * q + 2], nrm[:, 4 * q:4 * q + 2], -1.0, None, ALU.mult
                                 ).then_inc(s_ready, 1)

            def weights(u):
                h, q = u // 2, u % 2
                w = P * (q + 1)
                dve.wait_ge(e_ready, 2 * (u + 1))
                c = nrm[:, 16 + 4 * q:18 + 4 * q]
                link(V_.reciprocal(c, nrm[:, 4 * q + 2:4 * q + 4]))
                g0 = q * WIN_REST + h * 3
                link(V_.tensor_tensor(c, c, gates[:, g0 + 1:g0 + 3], ALU.mult))
                V_.tensor_tensor(eA[q][:, :, 0:w], eA[q][:, :, 0:w], c.unsqueeze(2).broadcast_to((P, 2, w)), ALU.mult
                                 ).then_inc(p_ready, 1)

            def take_turned(u):
                q = u % 2
                k = att_use(u, 1)
                dve.wait_ge(aux_done, k + 1)
                if u >= 2:
                    dve.wait_ge(pv_done, u - 1)
                n = 2 * (q + 1)
                V_.tensor_copy(pA[q][:, 0:n, :], aux(k)[:, 0:n * P].rearrange("p (n s) -> p n s", n=n)
                               ).then_inc(aux_evac[k % 4], 1)

            def take_out(hp):
                dve.wait_ge(pv_done, 4 * hp + 4)
                V_.tensor_copy(oTv[:, 8 + hp, :], banks[hp % 2][:, 0:S]).then_inc(pv_evac, 1)

            for u in range(33):
                if u < 32:
                    logits(u)
                if u >= 1:
                    weights(u - 1)
                    take_turned(u - 1)
                    if u >= 5 and (u - 5) % 4 == 0:
                        take_out((u - 5) // 4)
            take_out(7)

            residual(J_WOUT, 1, 2)
            for u in range(4):
                k = X["skt"] + u
                dve.wait_ge(aux_done, k + 1)
                V_.tensor_copy(skT[:, 4 * u:4 * u + 4, :], aux(k)[:, :].rearrange("p (n s) -> p n s", n=4)
                               ).then_inc(aux_evac[k % 4], 1)
            rms(4)
            scale_rows()
            take_transposed(X["norm3"], 3)
            dve.wait_ge(gbc_landed, 32)
            for m in range(MT):
                V_.tensor_tensor(xn[:, m, :], tm[:, m, :], gbc[:, :], ALU.mult).then_inc(xn_ready, 1)

            for m in range(MT):
                wait_aux_evac(dve, X["psc"] + 4 * m + 3)
                for f in range(16):
                    last = V_.max(topv[:, f, 0:8], sc[:, f, :])
                link(last)
                for f in range(16):
                    V_.max_index(topi[:, f, 0:8], topv[:, f, 0:8], sc[:, f, :])
                for f in range(16):
                    last = V_.match_replace(scw[:, f, :], topv[:, f, 0:8], sc[:, f, :], -3e38)
                link(last)
                for f in range(16):
                    last = V_.max(topv[:, f, 8:16], scw[:, f, :])
                link(last)
                for f in range(16):
                    last = V_.max_index(topi[:, f, 8:16], topv[:, f, 8:16], scw[:, f, :])
                link(last)
                link(V_.tensor_copy(topf, topi))
                t4 = topv[:, :, :].rearrange("p (h b) k -> p h b k", b=2)
                for h in range(PH):
                    last = V_.tensor_tensor(cand[:, h, :].rearrange("p (i j) -> p i j", i=TOPK),
                                            t4[:, h, 0, :].unsqueeze(2).broadcast_to((P, TOPK, TOPK)),
                                            t4[:, h, 1, :].unsqueeze(1).broadcast_to((P, TOPK, TOPK)), ALU.add)
                link(last)
                for h in range(PH):
                    last = V_.max(bv[:, h, 0:8], cand[:, h, :])
                link(last)
                for h in range(PH):
                    V_.max_index(bp[:, h, 0:8], bv[:, h, 0:8], cand[:, h, :])
                for h in range(PH):
                    last = V_.match_replace(candw[:, h, :], bv[:, h, 0:8], cand[:, h, :], -3e38)
                link(last)
                for h in range(PH):
                    last = V_.max(bv[:, h, 8:16], candw[:, h, :])
                link(last)
                for h in range(PH):
                    last = V_.max_index(bp[:, h, 8:16], bv[:, h, 8:16], candw[:, h, :])
                link(last)
                f4 = topf[:, :, :].rearrange("p (h b) k -> p h b k", b=2)
                for part, op, arg, res in ((0, ALU.logical_shift_right, 4, i1), (1, ALU.bitwise_and, 15, i2)):
                    link(V_.tensor_scalar(pq, bp, arg, None, op))
                    link(V_.tensor_copy(pf, pq[:, :, :].rearrange("p h k -> p (h k)")))
                    link(V_.tensor_tensor(oh, pf.unsqueeze(2).broadcast_to((P, SLOTS, TOPK)),
                                          iota16.unsqueeze(1).broadcast_to((P, SLOTS, TOPK)), ALU.is_equal))
                    oh4 = oh[:, :, :].rearrange("p (h k) t -> p h k t", h=PH)
                    for h in range(PH):
                        last = V_.tensor_tensor(oh4[:, h], oh4[:, h], f4[:, h, part, :].unsqueeze(1).broadcast_to(
                            (P, TOPK, TOPK)), ALU.mult)
                    link(last)
                    link(V_.tensor_reduce(res, oh, AX_X, ALU.add))
                V_.scalar_tensor_tensor(idx[:, m * SLOTS:(m + 1) * SLOTS], i1, float(NK), i2, ALU.mult, ALU.add
                                        ).then_inc(idx_ready, 1)
                link(V_.tensor_copy(bs[:, 0:PH], bv[:, :, 0]))
                V_.tensor_tensor(bv, bv, bs[:, 0:PH].unsqueeze(2).broadcast_to((P, PH, TOPK)), ALU.subtract
                                 ).then_inc(best_shift, 1)
                dve.wait_ge(best_exp, m + 1)
                link(V_.tensor_reduce(bs[:, 8:16], bv, AX_X, ALU.add))
                link(V_.reciprocal(bs[:, 16:24], bs[:, 8:16]))
                V_.tensor_tensor(gts[:, m * SLOTS:(m + 1) * SLOTS].rearrange("p (h k) -> p h k", h=PH), bv,
                                 bs[:, 16:24].unsqueeze(2).broadcast_to((P, PH, TOPK)), ALU.mult).then_inc(routed, 1)
            V_.memset(accx, 0.0).then_inc(acc_zero, 1)
            dve.wait_ge(acc_zero, 1)
            dve.wait_ge(routed, MT)
            dve.wait_ge(xn_ready, MT)

            per = SLOTS // (GROUPS * EG)
            for m in range(MT):
                with dve.Fori(0, per) as i:
                    def dots(g):
                        dve.wait_ge(u_landed[g], 16 * EG * (m * per + 1) + i * (16 * EG))
                        for b in range(EG):
                            V_.tensor_tensor_reduce(out=ubuf[g][b], in0=ubuf[g][b], in1=xn[:, m, :], scale=1.0,
                                                    scalar=0.0, op0=ALU.mult, op1=ALU.add,
                                                    accum_out=hcur[:, g * EG + b:g * EG + b + 1]
                                                    ).then_inc(dots_done[g], 1)

                    def adds(g):
                        dve.wait_ge(gelu_done[g], m * per + 1 + i)
                        V_.tensor_tensor(wcur[:, g * EG:(g + 1) * EG], hgel[:, g * EG:(g + 1) * EG],
                                         gts[:, bass.ds(i * (GROUPS * EG) + (m * SLOTS + g * EG), EG)], ALU.mult
                                         ).then_inc(w_done, 1)
                        dve.wait_ge(w_done, GROUPS * m * per + g + 1 + i * GROUPS)
                        dve.wait_ge(v_landed[g], 16 * EG * (m * per + 1) + i * (16 * EG))
                        for b in range(EG):
                            V_.scalar_tensor_tensor(accx[:, m, :], vbuf[g][b], wcur[:, g * EG + b:g * EG + b + 1],
                                                    accx[:, m, :], ALU.mult, ALU.add).then_inc(v_done[g], 1)
                            dve.wait_ge(v_done[g], EG * m * per + EG + b + 1 + i * EG)

                    dots(0)
                    for g in range(1, GROUPS):
                        dots(g)
                        adds(g - 1)
                    adds(GROUPS - 1)
            for m in range(MT):
                V_.tensor_tensor(xr[:, m, :], xr[:, m, :], accx[:, m, :], ALU.add).then_inc(peer_added, 1)
            rms(5)
            scale_rows()
            k = X["pt"]
            dve.wait_ge(aux_done, k + 1)
            V_.tensor_copy(pT, aux(k)[:, :].rearrange("p (c s) -> p c s", c=2)).then_inc(aux_evac[k % 4], 1)
            take_transposed(X["norm4"], 4)
            for n in range(NT):
                wait_acc_evac(dve, A_GATE + n)
                for m in range(MT):
                    s = sg[n % 2][m]
                    k = X["pp"] + 2 * n + m
                    dve.wait_ge(aux_done, k + 1)
                    V_.tensor_tensor(s, s, aux(k)[:, :], ALU.mult).then_inc(aux_evac[k % 4], 1)
                    wait_aux_evac(dve, k)
                    V_.tensor_tensor(xr[:, m, n * 512:n * 512 + 512], xr[:, m, n * 512:n * 512 + 512], s, ALU.add
                                     ).then_inc(out_ready, 1)

        @block.tensor
        def _(pe):
            def acc_free(n, more):
                pe.wait_ge(acc_evac[n % 2], 2 * (n // 2) + 2 + more)

            def rows_job(j, n, x=None, width=512, first=True, last=True, k0=0, jm=0, am=0):
                x = aTv if x is None else x
                if first:
                    acc_free(n, am)
                for q in range(4):
                    s = 4 * (j % 2) + q
                    pe.wait_ge(w_landed[s], landed(j, q, jm))
                    for c in range(4):
                        for m in range(MT):
                            mm = nc.tensor.matmul(banks[2 * (n % 2) + m][:, 0:width],
                                                  x[:, k0 + 4 * q + c, m * P:(m + 1) * P], slot[s][:, c, 0:width],
                                                  start=first and q == 0 and c == 0, stop=last and q == 3 and c == 3)
                    mm.then_inc(slots_free, 1)

            def cols_job(j, n, jm=0, am=0):
                acc_free(n, am)
                for q in range(4):
                    s = 4 * (j % 2) + q
                    pe.wait_ge(w_landed[s], landed(j, q, jm))
                    for c in range(4):
                        for b in range(4):
                            mm = nc.tensor.matmul(banks[2 * (n % 2) + b // 2][:, (b % 2) * S:(b % 2 + 1) * S],
                                                  slot[s][:, c, b * P:(b + 1) * P], aTv[:, 4 * q + c, :],
                                                  start=q == 0 and c == 0 and b % 2 == 0, stop=q == 3 and c == 3,
                                                  skip_group_check=True)
                    mm.then_inc(slots_free, 1)

            def turn(k, pairs):
                for n, (col, src) in enumerate(pairs):
                    mm = nc.tensor.transpose(aux(k)[:, col:col + P], src, ident)
                mm.then_inc(aux_done, 1)

            def turn_stream(k0, norm):
                pe.wait_ge(scaled, 2 * (norm + 1))
                for u in range(8):
                    wait_aux_free(pe, k0 + u)
                    turn(k0 + u, [((2 * c + m) * P, tm[:, m, (2 * u + c) * P:(2 * u + c + 1) * P])
                                  for c in range(2) for m in range(MT)])
                wait_aux_evac(pe, k0 + 7)

            for pair in acc_evac:
                pe.sem_inc(pair, 2)
            pe.wait_ge(cst_landed, 16)
            pe.wait_ge(gain_landed, 16 * 5)
            nc.tensor.transpose(aux(0)[:, 0:80], tmp[0:80, 0:P], ident[0:80, 0:80]).then_inc(aux_done, 1)
            turn_stream(X["norm0"], 0)

            def sb_scores(g, i):
                wait_acc_evac(pe, A_QKV + 3 * g, i * 6)
                wait_acc_evac(pe, A_QKV + 3 * g + 1, i * 6)
                for h in range(4):
                    k = X["sb"] + 12 * g + h
                    wait_aux_free(pe, k, i * 6)
                    nc.tensor.matmul(aux(k)[:, 0:S], kT[:, h, 0:P], qT[:, h, :], start=True, stop=True)
                    nc.tensor.matmul(aux(k)[:, S:TRI_W], kT[:, h, P:S], qT[:, h, P:S], start=True, stop=True
                                     ).then_inc(aux_done, 1)

            def sb_suffix(g, i):
                pe.wait_ge(sp_ready, g + 1 + i * 2)
                for h in range(4):
                    k = X["sb"] + 12 * g + 4 + h
                    nc.tensor.matmul(aux(k)[:, 0:TRI_W], tri, sp[:, h, :], start=True, stop=False)
                    nc.tensor.matmul(aux(k)[:, P:S], ones, sp[:, h, S:TRI_W], start=False, stop=True
                                     ).then_inc(aux_done, 1)

            def sb_values(g, i):
                pe.wait_ge(at_ready, g + 1 + i * 2)
                wait_acc_evac(pe, A_QKV + 3 * g + 2, i * 6)
                for h in range(4):
                    k = X["sb"] + 12 * g + 8 + h
                    nc.tensor.matmul(aux(k)[:, 0:S], V[:, 0, h * P:(h + 1) * P], at[:, h, 0:S], start=True, stop=False)
                    nc.tensor.matmul(aux(k)[:, P:S], V[:, 1, h * P:(h + 1) * P], at[:, h, S:TRI_W], start=False,
                                     stop=True).then_inc(aux_done, 1)

            with pe.Fori(0, 2) as i:
                for g in range(2):
                    n = 3 * g
                    cols_job(J_QKV + n, A_QKV + n, jm=i * 3, am=i * 6)
                    if g == 1:
                        sb_values(0, i)
                    cols_job(J_QKV + n + 1, A_QKV + n + 1, jm=i * 3, am=i * 6)
                    sb_scores(g, i)
                    rows_job(J_QKV + n + 2, A_QKV + n + 2, jm=i * 3, am=i * 6)
                    sb_suffix(g, i)
                sb_values(1, i)
            wait_aux_evac(pe, X["sb"] + 47)
            with pe.Fori(0, 2) as i:
                for n in range(2):
                    rows_job(J_WO + n, A_WO + n, x=oTv, jm=i, am=i * 2)
            turn_stream(X["norm1"], 1)

            with pe.Fori(0, 8) as i:
                for n in range(2):
                    cols_job(J_W1 + n, A_W1 + n, jm=i, am=i * 2)
            pe.wait_ge(h_ready, D_FF // P // 2)
            with pe.Fori(0, 2) as i:
                for n in range(2):
                    for kq in range(4):
                        rows_job(J_W2 + 4 * n + kq, A_W2 + n, x=hT, k0=16 * kq, first=kq == 0, last=kq == 3,
                                 jm=i * 4, am=i * 2)
            turn_stream(X["norm2"], 2)

            def flips(piece):
                pe.wait_ge(xp_landed[piece % 2], 16 * (piece // 2 + 1))
                for f in range(3):
                    k = X["flip"] + 3 * piece + f
                    wait_aux_free(pe, k)
                    nc.tensor.matmul(aux(k)[:, :], flip, tmp[:, (piece % 2) * 1536 + f * 512:(piece % 2) * 1536 + f * 512 + 512],
                                     start=True, stop=True).then_inc(aux_done, 1)

            for n in range(8):
                rows_job(J_WIN + n, A_WIN + n, width=512 if n < 7 else WIN_REST)
                if n == 0:
                    pe.wait_ge(mask_row, 1)
                    pe.wait_ge(small_landed, 16 * 8)
                    pe.wait_ge(oh_landed, 16)
                    wait_aux_free(pe, X["line"])
                    nc.tensor.matmul(aux(X["line"])[0:16, :], relb[0:33, :], gbc[0:33, 512:1024], start=True, stop=True
                                     ).then_inc(aux_done, 1)
                if n == 2 or n == 4:
                    flips(n - 2)
                    flips(n - 1)
            pe.wait_ge(qk_norm, 1)
            for u in range(4):
                wait_aux_free(pe, X["qt"] + u)
                turn(X["qt"] + u, [((2 * c + m) * P, big[:, 2048 + m * 1024 + (2 * u + c) * P:2048 + m * 1024 + (2 * u + c + 1) * P])
                                   for c in range(2) for m in range(MT)])
            pe.wait_ge(qk_norm, 2)
            for u in range(2):
                wait_aux_free(pe, X["kt"] + u)
                turn(X["kt"] + u, [((2 * j + m) * P, kn[:, u, m, j * P:(j + 1) * P]) for j in range(2) for m in range(MT)])
            wait_acc_evac(pe, A_WIN + 4)
            for u in range(2):
                wait_aux_free(pe, X["ct"] + u)
                turn(X["ct"] + u, [((2 * c + m) * P, kvc[:, m, (2 * u + c) * P:(2 * u + c + 1) * P])
                                   for c in range(2) for m in range(MT)])
            wait_acc_evac(pe, A_WIN + 1)
            wait_acc_evac(pe, A_WIN + 0)
            for q in range(4):
                pe.wait_ge(w_landed[4 + q], landed(J_MISC, q))
            band = v3(ring, 5 * 2048, 4, TRI_W)
            poolw = v3(ring, 4 * 2048, 8, 256)
            w2c = [v3(ring, 6 * 2048 + v * P, 2, DK) for v in range(2)]
            for u in range(4):
                k = X["mixed"] + u
                wait_aux_free(pe, k)
                for c in range(2):
                    cb = 2 * u + c
                    nc.tensor.matmul(aux(k)[:, c * S:(c + 1) * S], U[:, 0, cb * P:(cb + 1) * P], band[:, u, 0:S],
                                     start=True, stop=False)
                    mm = nc.tensor.matmul(aux(k)[:, c * S + P:(c + 1) * S], U[:, 1, cb * P:(cb + 1) * P],
                                          band[:, u, S:TRI_W], start=False, stop=True)
                mm.then_inc(aux_done, 1)
            wait_aux_evac(pe, X["mixed"] + 3)
            for g in range(4):
                k = X["pool"] + g
                wait_aux_free(pe, k)
                for d in range(2):
                    for c in range(2):
                        mm = nc.tensor.matmul(aux(k)[:, d * S:(d + 1) * S], poolw[:, 2 * g + c, d * P:(d + 1) * P],
                                              mixT[:, 2 * g + c, :], start=c == 0, stop=c == 1)
                mm.then_inc(aux_done, 1)
            pe.wait_ge(pads_ready, 1)
            pe.wait_ge(flat_ready, 1)
            for q in range(4):
                pe.wait_ge(w_landed[q], landed(J_CMP, q))
            for v in range(2):
                k = X["hid"] + v
                wait_aux_free(pe, k)
                rows = slice(v * DK, (v + 1) * DK)
                for h in range(2):
                    for l in range(CMP_L):
                        w1 = v3(ring, (l // 8) * 2048, 8, CMP_H)[rows, l % 8, h * P:(h + 1) * P]
                        mm = nc.tensor.matmul(aux(k)[:, h * P:(h + 1) * P], w1, aT[rows, l * P:(l + 1) * P],
                                              start=l == 0, stop=l == CMP_L - 1)
                mm.then_inc(aux_done, 1)
            wait_aux_evac(pe, X["hid"] + 1)
            k = X["cmp"]
            wait_aux_free(pe, k)
            for v in range(2):
                for h in range(2):
                    mm = nc.tensor.matmul(aux(k)[:, v * DK:(v + 1) * DK], hc[:, v, h, :], w2c[v][:, h, :],
                                          start=h == 0, stop=h == 1)
            mm.then_inc(aux_done, 1)
            wait_aux_evac(pe, k)
            wait_aux_free(pe, X["kct"])
            turn(X["kct"], [(0, big[:, 3968:4096])])
            pe.sem_inc(slots_free, 8)
            wait_aux_evac(pe, X["kct"])
            for l in range(2):
                k = X["csc"] + l
                rows = slice(l * DK, (l + 1) * DK)
                wait_aux_free(pe, k)
                for q in range(MT):
                    for r in range(R):
                        for j in range(2):
                            o = q * P + (2 * r + j) * CPAD
                            mm = nc.tensor.matmul(aux(k)[:, o:o + CPAD], qTa[rows, 4 * j + r, q * P:(q + 1) * P],
                                                  kcT[rows, 32 * (2 * j + l):32 * (2 * j + l) + CPAD], start=True, stop=True)
                mm.then_inc(aux_done, 1)
            pe.wait_ge(pc_ready, 1)
            for q in range(MT):
                k = X["pct"] + q
                wait_aux_free(pe, k)
                turn(k, [(r * P, Pc3[:, 4 * q + r, :]) for r in range(R)])

            def att_logits(u):
                h, q = u // 2, u % 2
                g, r = h // R, h % R
                rows = slice((g % 2) * DK, (g % 2 + 1) * DK)
                w = P * (q + 1)
                k = att_use(u, 0)
                wait_aux_free(pe, k)
                for b in range(2):
                    mm = nc.tensor.matmul(aux(k)[:, b * S:b * S + w], qTa[rows, R * (g // 2) + r, q * P:(q + 1) * P],
                                          kTn[rows, b, g // 2, 0:w], start=True, stop=True)
                mm.then_inc(aux_done, 1)

            def att_turn(u):
                q = u % 2
                k = att_use(u, 1)
                pe.wait_ge(p_ready, u + 1)
                wait_aux_free(pe, k)
                turn(k, [((b * (q + 1) + t) * P, eA[q][:, b, t * P:(t + 1) * P]) for b in range(2) for t in range(q + 1)])

            def att_values(u):
                h, q = u // 2, u % 2
                g, r, hp = h // R, h % R, h // 2
                if u % 4 == 0 and hp >= 2:
                    pe.wait_ge(pv_evac, hp - 1)
                wait_aux_evac(pe, att_use(u, 1))
                o = banks[hp % 2][(h % 2) * DK:(h % 2 + 1) * DK, q * P:(q + 1) * P]
                nc.tensor.matmul(o, Vcm[:, g, :], PcT[:, R * q + r, :], start=True, stop=False)
                for b in range(2):
                    for t in range(q + 1):
                        mm = nc.tensor.matmul(o, vn[:, b, t, g * DK:(g + 1) * DK], pA[q][:, b * (q + 1) + t, :],
                                              start=False, stop=b == 1 and t == q)
                mm.then_inc(pv_done, 1)

            wait_aux_evac(pe, X["pct"] + 1)
            for u in range(34):
                if u < 32:
                    att_logits(u)
                if 1 <= u <= 32:
                    att_turn(u - 1)
                if u >= 2:
                    att_values(u - 2)
            pe.wait_ge(pv_evac, 8)
            with pe.Fori(0, 2) as i:
                for n in range(2):
                    rows_job(J_WOUT + n, A_WOUT + n, x=oTv, jm=i, am=i * 2)
            pe.wait_ge(sk_landed, 16)
            for u in range(4):
                wait_aux_free(pe, X["skt"] + u)
                turn(X["skt"] + u, [(n * P, sk[:, 4 * u + n, :]) for n in range(4)])
            turn_stream(X["norm3"], 3)

            with pe.Fori(0, 2) as i:
                for n in range(2):
                    cols_job(J_WQ + n, A_WQ + n, jm=i, am=i * 2)
            wait_acc_evac(pe, A_WQ + 2)
            wait_acc_evac(pe, A_WQ + 3)
            for m in range(MT):
                for n in range(4):
                    k = X["psc"] + 4 * m + n
                    wait_aux_free(pe, k)
                    for f in range(4):
                        mm = nc.tensor.matmul(aux(k)[:, f * P:(f + 1) * P], qpT[:, 4 * n + f, m * P:(m + 1) * P],
                                              skT[:, 4 * n + f, :], start=True, stop=True)
                    mm.then_inc(aux_done, 1)

            pe.wait_ge(ple_landed, 32)
            wait_aux_free(pe, X["pt"])
            turn(X["pt"], [((2 * c + m) * P, pin[:, m, c * P:(c + 1) * P]) for c in range(2) for m in range(MT)])
            turn_stream(X["norm4"], 4)
            for n in range(NT):
                rows_job(J_GATE + n, A_GATE + n)
                for m in range(MT):
                    k = X["pp"] + 2 * n + m
                    wait_aux_free(pe, k)
                    for c in range(2):
                        mm = nc.tensor.matmul(aux(k)[:, :], pT[:, c, m * P:(m + 1) * P], plew[:, c, n * 512:n * 512 + 512],
                                              start=c == 0, stop=c == 1)
                    mm.then_inc(aux_done, 1)

        @block.gpsimd
        def _(pool):
            nc.gpsimd.memset(idxc[:, :], 0).then_inc(slots_free, 8)
            pool.wait_ge(slots_free, used(J_WIN + 7))
            nc.gpsimd.memset(flat[:, :, :, NCMP:], 0.0).then_inc(pads_ready, 1)
            wait_aux_evac(pool, X["qt"] + 3)
            nc.gpsimd.memset(big[:, 3584:3840], 0.0).then_inc(pads_ready, 1)
            pool.wait_ge(routed, MT)
            pool.wait_ge(idx_ready, MT)
            pool.wait_ge(slots_free, used(J_WQ + 3))
            per = SLOTS // (GROUPS * EG)
            for g in range(GROUPS):
                pool.sem_inc(v_done[g], EG)
            for m in range(MT):
                with pool.Fori(0, per) as i:
                    for g in range(GROUPS):
                        pool.wait_ge(v_done[g], EG * m * per + EG + i * EG)
                        nc.gpsimd.tensor_copy(idxc[:, g * EG:(g + 1) * EG],
                                              idx[:, bass.ds(i * (GROUPS * EG) + (m * SLOTS + g * EG), EG)]
                                              ).then_inc(idx_copied, 1)
                        pool.wait_ge(idx_copied, 1)
                        pool.sem_clear(idx_copied)
                        for tab, buf, landed_ in ((a["peer_u"], ubuf, u_landed), (a["peer_v"], vbuf, v_landed)):
                            for b in range(EG):
                                nc.gpsimd.indirect_dma_start(
                                    out=buf[g][b], out_offset=None, in_=tab,
                                    in_offset=bass.IndirectOffsetOnAxis(ap=idxc[:, g * EG + b:g * EG + b + 1], axis=0),
                                ).then_inc(landed_[g], 16)


_SQUEEZE = {"x": "x", "sb_w_qkv": "sb_w_qkv", "sb_w_o": "sb_w_o", "norm_mix": "norm_mix", "norm_mlp": "norm_mlp",
            "mlp_w1": "mlp_w1", "mlp_w2": "mlp_w2", "p": "p_2", "mix_norm_w": "mix_norm_w_2", "w_in": "w_in_2",
            "q_norm_w": "q_norm_w_2", "k_norm_w": "k_norm_w_2", "cmp_k_pos": "cmp_k_pos_2", "cmp_k_w1": "cmp_k_w1_2",
            "cmp_k_b1": "cmp_k_b1_2", "cmp_k_w2": "cmp_k_w2_2", "cmp_v_pos": "cmp_v_pos_2", "cmp_v_w1": "cmp_v_w1_2",
            "cmp_v_b1": "cmp_v_b1_2", "cmp_v_w2": "cmp_v_w2_2", "pool_w": "pool_w_2", "pool_scale": "pool_scale_2",
            "w_out": "w_out_2", "ffn_norm_w": "ffn_norm_w_2", "peer_w_q": "peer_w_q_2",
            "peer_sub_keys": "peer_sub_keys_2", "peer_u": "peer_u_2", "peer_v": "peer_v_2",
            "ple_norm_w": "ple_norm_w_2", "ple_w_gate": "ple_w_gate_2", "ple_w_proj": "ple_w_proj_2"}
_WHOLE = {"final_norm": "final_norm", "rel_bias": "rel_bias_2"}


def kernel(**inputs):
    import concourse.bacc as bacc
    from concourse.bass_utils import run_bass_kernel_spmd

    nc = bacc.Bacc("TRN2", target_bir_lowering=False, num_devices=1)
    arrays, aps = {}, {}

    def give(name, x):
        x = np.ascontiguousarray(x)
        arrays[f"in_{name}"] = x
        aps[name] = nc.dram_tensor(f"in_{name}", x.shape, mybir.dt.from_np(x.dtype), kind="ExternalInput").ap()

    for name, given in _SQUEEZE.items():
        x = np.asarray(inputs[given])
        give(name, x.reshape(x.shape[2:] if name == "p" else x.shape[1:]))
    for name, given in _WHOLE.items():
        give(name, inputs[given])
    for name, x in host_constants().items():
        give(name, x)
    out = nc.dram_tensor("out", (S, D), F32, kind="ExternalOutput").ap()
    line_dram = nc.dram_tensor("line", (16, 512), F32, kind="Internal").ap()
    build(nc, aps, out, line_dram)
    r = run_bass_kernel_spmd(nc, [arrays], core_ids=[0])
    return r.results[0]["out"].reshape(1, S, D)
```

```python
from contextlib import ExitStack

import numpy as np
import concourse.bass as bass
from concourse import mybir

P = 128
F32 = mybir.dt.float32
U32 = mybir.dt.uint32
ALU = mybir.AluOpType
ACT = mybir.ActivationFunctionType
AX_X = mybir.AxisListType.X

S = 256
D = 2048
MT = S // P
KC = D // P
NT = D // 512
EPS = 1e-6
NEG = -1e30

SB_HEADS = 16
SB_SCALE = (D // SB_HEADS) ** -0.5
SB_GROUPS = 4
TRI_W = 384

D_FF = 8192
G, R, DK = 4, 4, 64
CMP_L, CMP_S, CMP_H = 32, 16, 256
NCMP = S // CMP_S - CMP_L // CMP_S + 1
CPAD = 16
POOL_W = 1024
WIN_REST = 48
PH, NK, TOPK = 8, 128, 16
SLOTS = PH * TOPK
EG = 2
GROUPS = 4

J_QKV, J_WO, J_W1, J_W2, J_W1B, J_W2B, J_WIN = 0, 12, 16, 24, 32, 40, 48
J_CMP, J_WOUT, J_WQ, J_GATE = 56, 57, 61, 65
A_QKV, A_WO, A_W1, A_W2, A_W1B, A_W2B, A_WIN, A_WOUT, A_WQ, A_GATE = 0, 12, 16, 24, 28, 36, 40, 48, 52, 56
H_NORM0, H_O, H_NORM1, H_NORM2, H_MIX, H_NORM3, H_NORM4 = 0, 16, 20, 36, 52, 68, 84
_uses = [("gain", 1), ("norm0", 8), ("sb", 48), ("norm1", 8), ("norm2", 8), ("line", 1), ("flip", 12),
         ("qt", 4), ("kt", 2), ("ct", 2), ("mixed", 4), ("pool", 4), ("hid", 2), ("cmp", 1), ("kct", 1),
         ("csc", 2), ("pct", 2), ("att", 64), ("skt", 4), ("norm3", 8), ("psc", 8), ("pt", 1), ("norm4", 8),
         ("pp", 8)]
X = {}
_n = 0
for _name, _count in _uses:
    X[_name] = _n
    _n += _count


def landed(j, q, d=0):
    return 16 * (j + 1 + (j >= J_CMP)) + 16 * d


def used(j, d=0):
    return 4 + 8 * (j + 1) + 8 * d


def att_use(u, turned):
    return X["att"] + (min(2 * u + 2, 63) if turned else max(2 * u - 1, 0))


def host_constants():
    k, q = np.arange(P)[:, None], np.arange(P)[None, :]
    ident = (k == q).astype(np.float32)
    tri = (k >= q).astype(np.float32)
    ones = np.ones((P, P), np.float32)
    flip = (k + q == P - 1).astype(np.float32)
    strict = np.where(k < q, 0.0, NEG).astype(np.float32)
    neg = np.concatenate([strict, np.zeros((P, P), np.float32), strict], axis=1)
    iota = np.broadcast_to(np.arange(TOPK, dtype=np.float32), (P, TOPK))
    cst = np.concatenate([ident, tri, ones, flip, neg, iota], axis=1)
    band = np.zeros((S, 4, S), np.float32)
    for g, w in enumerate((2, 4, 8, 16)):
        for t in range(S):
            lo = max(t + 1 - w, 0)
            band[lo:t + 1, g, t] = np.float32(1.0) / np.float32(t + 1 - lo)
            band[t, g, t] -= 1.0
    band = np.concatenate([band[:P], band[P:, :, P:]], axis=2)
    onehot = np.zeros((33, 512), np.float32)
    for y in range(511):
        rel = 255 - y
        if rel < 0:
            onehot[32, y] = 1.0
        elif rel < 16:
            onehot[rel, y] = 1.0
        else:
            large = 16 + int(np.float32(np.log(np.float32(rel) / np.float32(16))) / np.float32(np.log(128 / 16)) * np.float32(16))
            onehot[min(large, 31), y] = 1.0
    onehot[32, 511] = 1.0
    return {"cst": np.ascontiguousarray(cst), "band": np.ascontiguousarray(band), "onehot": onehot}


def build(nc, a, out, line_dram):
    with ExitStack() as ctx:
        def sem(name):
            return ctx.enter_context(nc.semaphore(name))

        placed = [(nc.sbuf_base + 63) // 64 * 64]

        def place(name, cols, dt=F32, offset=None):
            at_ = placed[0] if offset is None else offset
            if offset is None:
                placed[0] += (4 * cols + 31) // 32 * 32
            t = nc.alloc_sbuf_tensor_at(name, [P, cols], dt, offset=at_)
            return t, at_

        F32R = mybir.dt.float32r
        raw, raw_at = place("raw", 4 * 2048)
        wh, wh_at = place("wh", 4 * 1024, F32R)
        wl, _ = place("wl", 4 * 1024, F32R)
        vrows, _ = place("vrows", 16384, offset=raw_at)
        mrows, _ = place("mrows", 8192, offset=wh_at)
        Ah, ah_at = place("Ah", KC * S, F32R)
        Al, al_at = place("Al", KC * S, F32R)
        eacc, _ = place("eacc", MT * D, offset=ah_at)
        best, _ = place("best", KC * S, offset=al_at)
        big, big_at = place("big", 16384)
        hTh, _ = place("hTh", 32 * S, F32R, offset=big_at)
        hTl, _ = place("hTl", 32 * S, F32R, offset=big_at + 4 * 32 * S)
        x_res, _ = place("x_res", MT * D)
        tmp, _ = place("tmp", MT * D)
        gbc, _ = place("gbc", D)
        cst, _ = place("cst", 4 * P + TRI_W + TOPK)
        gT = place("gT", 80)[0]
        ss = place("ss", MT * NT)[0]
        ms = place("ms", MT)[0]
        rt = place("rt", MT)[0]
        rstd = place("rstd", MT)[0]
        relb = place("relb", 16)[0]
        qnw = place("qnw", DK)[0]
        knw = place("knw", DK)[0]
        posT = place("posT", CMP_L)[0]
        b1c = place("b1c", 4)[0]
        psc = place("psc", 8)[0]
        gates = place("gates", MT * WIN_REST)[0]
        nrm = place("nrm", 3 * 64)[0]
        idx = gbc[:, 0:MT * SLOTS].bitcast(U32)
        gts = gbc[:, MT * SLOTS:2 * MT * SLOTS]
        idxc = place("idxc", GROUPS * EG, U32)[0]
        hcur = place("hcur", GROUPS * EG)[0]
        hgel = place("hgel", GROUPS * EG)[0]
        wcur = place("wcur", GROUPS * EG)[0]
        banks = [ctx.enter_context(nc.psum_tensor(f"bank{b}", [P, 512], F32)) for b in range(8)]

        ident, tri, ones, flip = (cst[:, n * P:(n + 1) * P] for n in range(4))
        neg = cst[:, 4 * P:4 * P + TRI_W]
        iota16 = cst[:, 4 * P + TRI_W:]

        def v3(t, o, x, y):
            return t[:, o:o + x * y].rearrange("p (x y) -> p x y", x=x)

        raw_half = [v3(raw, h * 1024, 2, 512) for h in range(8)]
        whv = [v3(wh, s * 1024, 2, 512) for s in range(4)]
        whf = [v3(wh[:, :].bitcast(F32), s * 1024, 2, 512) for s in range(4)]
        wlv = [v3(wl, s * 1024, 2, 512) for s in range(4)]
        Ahf = v3(Ah[:, :].bitcast(F32), 0, KC, S)
        hThf = hTh[:, :].bitcast(F32)
        xr = v3(x_res, 0, MT, D)
        tm = v3(tmp, 0, MT, D)
        Ah_v, Al_v = v3(Ah, 0, KC, S), v3(Al, 0, KC, S)
        A_ = (Ah_v, Al_v)
        H_ = (v3(hTh, 0, 32, S), v3(hTl, 0, 32, S))
        qT, kT, V = v3(big, 0, 4, S), v3(big, 1024, 4, S), v3(big, 2048, MT, 512)
        zm, ee, sp, at = (v3(big, 3072 + n * 1536, 4, TRI_W) for n in range(4))
        oraw = big[:, 9216:9216 + KC * S]
        U = v3(big, 0, MT, POOL_W)
        qn = big[:, 2048:4096].rearrange("p (m j r l d) -> p m j r l d", m=MT, j=2, r=R, l=2)
        qn3 = v3(big, 2048, MT * 16, DK)
        qTa = v3(big, 4096, 8, S)
        kvc = v3(big, 6144, MT, 512)
        kn = big[:, 7168:8192].rearrange("p (b m c) -> p b m c", b=2, m=MT)
        kn3 = v3(big, 7168, 16, DK)
        vn = big[:, 8192:9216].rearrange("p (b m c) -> p b m c", b=2, m=MT)
        kTn = big[:, 9216:10240].rearrange("p (b j s) -> p b j s", b=2, j=2)
        TB = v3(big, 10240, 16, TRI_W)
        cT = v3(big, 2048, G, S)
        hc = big[:, 3072:3584].rearrange("p (v h c) -> p v h c", v=2, h=2)
        Vcm = v3(big, 3584, G, DK)
        kcT = big[:, 3840:3968]
        kc2 = v3(big, 3968, 2, DK)
        flat = tmp[:, :].rearrange("p (l g c) -> p l g c", l=CMP_L, g=G)
        mixT = v3(gbc, 0, 8, S)
        csc = big[:, 0:512].rearrange("p (l q r j c) -> p l q r j c", l=2, q=MT, r=R, j=2)
        csc3 = v3(big, 0, 32, CPAD)
        cex3 = v3(big, 512, 32, CPAD)
        Pc = big[:, 1024:2048].rearrange("p (q r g c) -> p q r g c", q=MT, r=R, g=G)
        Pc3 = v3(big, 1024, 8, P)
        Xp = [v3(tmp, n * 1536, 4, TRI_W) for n in range(2)]
        sA = [v3(tmp, n * 512, 2, S) for n in range(2)]
        eA = [v3(tmp, 1024 + n * 512, 2, S) for n in range(2)]
        pA = [v3(tmp, 2048 + n * 512, 4, P) for n in range(2)]
        PcT = v3(tmp, 3072, 8, P)
        sk, skT = v3(big, 0, 16, P), v3(big, 2048, 16, P)
        qp = [v3(big, n * 1024, 4, S) for n in range(2)]
        scm = [v3(big, 4096 + m * 2048, 16, P) for m in range(MT)]
        scw = v3(big, 8192, 16, P)
        cand, candw = v3(big, 10240, PH, 256), v3(best, 2048, PH, 256)
        oh = v3(big, 14336, SLOTS, TOPK)
        topv = [v3(gbc, 512 + m * 512, 16, TOPK) for m in range(MT)]
        topi = [v3(gbc, 768 + m * 512, 16, TOPK).bitcast(U32) for m in range(MT)]
        topf = v3(best, 512, 16, TOPK)
        bv = v3(best, 768, PH, TOPK)
        bp = v3(best, 896, PH, TOPK).bitcast(U32)
        pq = v3(best, 1024, PH, TOPK).bitcast(U32)
        pf = best[:, 1152:1280]
        i1 = best[:, 1280:1408]
        i2 = best[:, 1408:1536]
        bs = best[:, 1536:1568]
        ubuf = [[big[:, s * 2048:(s + 1) * 2048] for s in pair] for pair in ((0, 1), (2, 6), (3, 4), (5, 7))]
        vbuf = [[vrows[:, (g * 2 + b) * 2048:(g * 2 + b + 1) * 2048] for b in range(EG)] for g in range(GROUPS)]
        xn = tm
        accx = v3(eacc, 0, MT, D)
        plew = v3(big, 0, 2, D)
        pin = v3(big, 4096, MT, 256)
        pT = v3(big, 4608, 2, S)
        sg = [[big[:, 5120 + (n * 2 + m) * 512:5120 + (n * 2 + m + 1) * 512] for m in range(MT)] for n in range(2)]

        w_landed = [sem(f"w_landed{s}") for s in range(4)]
        hi_done = sem("hi_done")
        split_done = sem("split_done")
        parts_used = sem("parts_used")
        a_hi = sem("a_hi")
        a_lo = sem("a_lo")
        misc_landed = sem("misc_landed")
        h_squared = sem("h_squared")
        h_hi = sem("h_hi")
        acc_evac = [sem("acc_evac0"), sem("acc_evac1")]
        aux_done = sem("aux_done")
        aux_evac = [sem(f"aux_evac{b}") for b in range(4)]
        cst_landed = sem("cst_landed")
        gain_landed = sem("gain_landed")
        x_landed = sem("x_landed")
        small_landed = sem("small_landed")
        gbc_landed = sem("gbc_landed")
        oh_landed = sem("oh_landed")
        line_stored = sem("line_stored")
        xp_landed = [sem("xp_landed0"), sem("xp_landed1")]
        sk_landed = sem("sk_landed")
        ple_landed = sem("ple_landed")
        sq_done = sem("sq_done")
        ms_ready = sem("ms_ready")
        rt_ready = sem("rt_ready")
        scaled = sem("scaled")
        x2_ready = sem("x2_ready")
        mask_row = sem("mask_row")
        w_done = sem("w_done")
        act_link = sem("act_link")
        dve_link = sem("dve_link")
        soft_ready = sem("soft_ready")
        sp_ready = sem("sp_ready")
        at_ready = sem("at_ready")
        h_ready = sem("h_ready")
        qk_norm = sem("qk_norm")
        pads_ready = sem("pads_ready")
        flat_ready = sem("flat_ready")
        head_ms = sem("head_ms")
        head_rt = sem("head_rt")
        cmp_shift = sem("cmp_shift")
        cmp_exp = sem("cmp_exp")
        pc_ready = sem("pc_ready")
        s_ready = sem("s_ready")
        e_ready = sem("e_ready")
        p_ready = sem("p_ready")
        pv_done = sem("pv_done")
        pv_evac = sem("pv_evac")
        xn_ready = sem("xn_ready")
        routed = sem("routed")
        best_shift = sem("best_shift")
        best_exp = sem("best_exp")
        idx_ready = sem("idx_ready")
        acc_zero = sem("acc_zero")
        idx_copied = sem("idx_copied")
        u_landed = [sem(f"u_landed{g}") for g in range(GROUPS)]
        v_landed = [sem(f"v_landed{g}") for g in range(GROUPS)]
        dots_done = [sem(f"dots_done{g}") for g in range(GROUPS)]
        gelu_done = [sem(f"gelu_done{g}") for g in range(GROUPS)]
        v_done = [sem(f"v_done{g}") for g in range(GROUPS)]
        peer_added = sem("peer_added")
        out_ready = sem("out_ready")
        stored = sem("stored")

        def aux(k):
            return banks[4 + k % 4]

        def wait_aux_free(pe, k, more=0):
            if k >= 4:
                pe.wait_ge(aux_evac[k % 4], k // 4 + more)

        def wait_aux_evac(eng, k, more=0):
            eng.wait_ge(aux_evac[k % 4], k // 4 + 1 + more)

        def wait_acc_evac(eng, n, more=0):
            eng.wait_ge(acc_evac[n % 2], 2 * (n // 2) + 4 + more)

        block = ctx.enter_context(nc.Block())

        @block.sync
        def _(sp):
            def unit(j, q, dst, src, wait=True, d=0):
                if wait:
                    sp.wait_ge(split_done, 8 * j + 2 * q + 2 + d * 8)
                sp.dma_start(dst, src).then_inc(w_landed[q], 16)

            def job(j, w, n0, k0=0, width=512, d=0):
                rows = w.rearrange("(c p) n -> p c n", p=P)
                for q in range(4):
                    unit(j, q, v3(raw, q * 2048, 4, 512)[:, :, 0:width],
                         rows[:, k0 + 4 * q:k0 + 4 * q + 4, bass.ds(n0, width)], d=d)

            sp.dma_start(xr, a["x"].rearrange("(m p) d -> p m d", p=P)).then_inc(x_landed, 16)
            with sp.Fori(0, 2) as i:
                for g in range(2):
                    for w in range(3):
                        job(J_QKV + 3 * g + w, a["sb_w_qkv"], i * 1024 + w * D + g * 512, d=i * 6)
            with sp.Fori(0, 2) as i:
                for n in range(2):
                    job(J_WO + n, a["sb_w_o"], i * 1024 + n * 512, d=i * 2)
            for half, (j1, j2) in enumerate(((J_W1, J_W2), (J_W1B, J_W2B))):
                with sp.Fori(0, 4) as i:
                    for n in range(2):
                        job(j1 + n, a["mlp_w1"], i * 1024 + (half * 4096 + n * 512), d=i * 2)
                with sp.Fori(0, 2) as i:
                    for n in range(2):
                        for kq in range(2):
                            job(j2 + 2 * n + kq, a["mlp_w2"], i * 1024 + n * 512, k0=32 * half + 16 * kq, d=i * 4)
            for n in range(8):
                job(J_WIN + n, a["w_in"], n * 512, width=512 if n < 7 else WIN_REST)
                if n == 0:
                    sp.wait_ge(x2_ready, 2)
                    sp.dma_start(gbc[0:33, 512:1024], a["onehot"]).then_inc(oh_landed, 16)
                if n == 2:
                    wait_aux_evac(sp, X["line"])
                    sp.dma_start(line_dram, gbc[0:16, 0:512]).then_inc(line_stored, 16)
                    sp.wait_ge(line_stored, 16)
                    for n4 in range(2):
                        sp.dma_start(Xp[n4], bass.AP(line_dram.tensor, n4 * 4 * 512, [[1, P], [512, 4], [1, TRI_W]])
                                     ).then_inc(xp_landed[n4], 16)
                if n == 4:
                    for n4 in range(2, 4):
                        wait_aux_evac(sp, X["flip"] + 3 * (n4 - 2) + 2)
                        sp.dma_start(Xp[n4 - 2], bass.AP(line_dram.tensor, n4 * 4 * 512, [[1, P], [512, 4], [1, TRI_W]])
                                     ).then_inc(xp_landed[n4 - 2], 16)
            for q in range(4):
                for v, name in enumerate(("cmp_k_w1", "cmp_v_w1")):
                    rows = a[name].rearrange("(l d) n -> d l n", d=DK)
                    unit(J_CMP, q, v3(raw, q * 2048, 8, CMP_H)[v * DK:(v + 1) * DK],
                         rows[:, 8 * q:8 * q + 8, :], v == 0)
            sp.wait_ge(parts_used, used(J_WIN + 7))
            sp.dma_start(v3(mrows, 0, 8, 256), a["pool_w"].rearrange("g (c p) d -> p (g c) d", p=P)
                         ).then_inc(misc_landed, 16)
            sp.dma_start(mrows[:, 2048:2048 + 4 * TRI_W], a["band"].rearrange("p g t -> p (g t)")
                         ).then_inc(misc_landed, 16)
            for v, name in enumerate(("cmp_k_w2", "cmp_v_w2")):
                sp.dma_start(v3(cst, P + v * P, 2, DK), a[name].rearrange("(h p) d -> p h d", p=P)
                             ).then_inc(misc_landed, 16)
            for base, w in ((J_WOUT, a["w_out"]), (J_WQ, a["peer_w_q"])):
                with sp.Fori(0, 2) as i:
                    for n in range(2):
                        job(base + n, w, i * 1024 + n * 512, d=i * 2)
                if base == J_WOUT:
                    sp.wait_ge(parts_used, used(J_WOUT))
                    sp.dma_start(sk, a["peer_sub_keys"].rearrange("h b k d -> k (h b) d")).then_inc(sk_landed, 16)
            rows = a["ple_w_gate"].rearrange("(c p) n -> p c n", p=P)
            for q in range(4):
                if q % 2 == 0:
                    sp.wait_ge(v_done[q // 2], MT * SLOTS // (GROUPS * EG) * EG + EG)
                unit(J_GATE, q, v3(raw, q * 2048, 4, 512), rows[:, 4 * q:4 * q + 4, 0:512])
            for g in range(2, GROUPS):
                sp.wait_ge(v_done[g], MT * SLOTS // (GROUPS * EG) * EG + EG)
            sp.dma_start(plew, a["ple_w_proj"].rearrange("(c p) n -> p c n", p=P)).then_inc(ple_landed, 16)
            sp.dma_start(pin, a["p"].rearrange("(m p) d -> p m d", p=P)).then_inc(ple_landed, 16)
            for n in range(1, 4):
                job(J_GATE + n, a["ple_w_gate"], n * 512)
            for n in range(NT):
                sp.wait_ge(out_ready, 2 * (n + 1))
                sp.dma_start(out.rearrange("(m p) d -> p m d", p=P)[:, :, n * 512:(n + 1) * 512],
                             xr[:, :, n * 512:(n + 1) * 512]).then_inc(stored, 16)
            sp.wait_ge(stored, 16 * NT)

        @block.scalar
        def _(act):
            links = [0]

            def link(ins):
                links[0] += 1
                ins.then_inc(act_link, 1)
                act.wait_ge(act_link, links[0])

            act.dma_start(cst[:, :], a["cst"]).then_inc(cst_landed, 16)
            for n, name in enumerate(("norm_mix", "norm_mlp", "mix_norm_w", "ffn_norm_w", "ple_norm_w")):
                act.dma_start(tmp[16 * n:16 * n + 16, 0:P], a[name].rearrange("(c p) -> c p", p=P)
                              ).then_inc(gain_landed, 16)
            act.dma_start(gbc[:, :], a["final_norm"].rearrange("(o d) -> o d", o=1).broadcast_to((P, D))
                          ).then_inc(gbc_landed, 16)
            with nc.allow_non_contiguous_dma(reason="small tables"):
                act.dma_start(relb[0:32, :], a["rel_bias"]).then_inc(small_landed, 16)
                act.dma_start(qnw[:, :], a["q_norm_w"].rearrange("(o d) -> o d", o=1).broadcast_to((P, DK))
                              ).then_inc(small_landed, 16)
                act.dma_start(knw[:, :], a["k_norm_w"].rearrange("(o d) -> o d", o=1).broadcast_to((P, DK))
                              ).then_inc(small_landed, 16)
                for v, name in enumerate(("cmp_k", "cmp_v")):
                    act.dma_start(posT[v * DK:(v + 1) * DK, :], a[name + "_pos"].rearrange("l d -> d l")
                                  ).then_inc(small_landed, 16)
                    act.dma_start(b1c[:, 2 * v:2 * v + 2], a[name + "_b1"].rearrange("(h p) -> p h", p=P)
                                  ).then_inc(small_landed, 16)
                act.dma_start(psc[:, :], a["pool_scale"].rearrange("(c p) -> p c", p=P)).then_inc(small_landed, 16)

            def squares(cols, piece):
                for m in range(MT):
                    nc.scalar.activation(tm[:, m, cols], xr[:, m, cols], ACT.Square,
                                         accum_out=ss[:, piece(m)]).then_inc(sq_done, 1)

            def all_squares():
                for n in range(NT):
                    squares(slice(n * 512, n * 512 + 512), lambda m: slice(m * NT + n, m * NT + n + 1))

            def root(n):
                act.wait_ge(ms_ready, n + 1)
                nc.scalar.activation(rt[:, :], ms[:, :], ACT.Sqrt).then_inc(rt_ready, 1)

            def conv(j, hq, d=0, width=512):
                act.wait_ge(w_landed[hq // 2], landed(j, hq // 2, d))
                act.wait_ge(parts_used, 8 * j + hq + 1 + d * 8)
                nc.scalar.copy(whv[hq % 4][:, :, 0:width], raw_half[hq][:, :, 0:width]).then_inc(hi_done, 1)

            def first(j, d=0, width=512):
                for hq in range(4):
                    conv(j, hq, d, width)

            def second(j, d=0, width=512, between=None):
                conv(j, 4, d, width)
                if between is not None:
                    between()
                for hq in range(5, 8):
                    conv(j, hq, d, width)

            def job_squares(a, n, i):
                wait_acc_evac(act, a, i * 2)
                squares(bass.ds(i * 1024 + n * 512, 512), lambda m: bass.ds(i * 2 + (m * NT + n), 1))

            def residual_jobs(j0, a0):
                with act.Fori(0, 2) as i:
                    for n in range(2):
                        second(j0 + n, i * 2)
                        first(j0 + n + 1, i * 2)
                        job_squares(a0 + n, n, i)

            def take_transposed(k0, gain):
                for c in range(KC):
                    act.wait_ge(aux_done, k0 + c // 2 + 1)
                    nc.scalar.activation(Ah_v[:, c, :], aux(k0 + c // 2)[:, (c % 2) * S:(c % 2 + 1) * S], ACT.Copy,
                                         scale=gT[:, 16 * gain + c:16 * gain + c + 1]).then_inc(a_hi, 1)

            act.wait_ge(x_landed, 16)
            wait_aux_evac(act, X["gain"])
            all_squares()
            root(0)
            first(J_QKV)
            take_transposed(X["norm0"], 0)

            with act.Fori(0, 2) as i:
                def weights_exp(g):
                    wait_aux_evac(act, X["sb"] + 12 * g + 7, i * 6)
                    nc.scalar.activation(at, at, ACT.Exp).then_inc(at_ready, 1)

                def softplus_log(g):
                    wait_aux_evac(act, X["sb"] + 12 * g + 3, i * 6)
                    nc.scalar.activation(ee, zm, ACT.Abs).then_inc(soft_ready, 1)
                    act.wait_ge(soft_ready, 3 * g + 1 + i * 6)
                    nc.scalar.activation(ee, ee, ACT.Exp, scale=-1.0).then_inc(soft_ready, 1)
                    act.wait_ge(soft_ready, 3 * g + 2 + i * 6)
                    nc.scalar.activation(ee, ee, ACT.Ln, bias=1.0).then_inc(soft_ready, 1)

                for g in range(2):
                    jq = J_QKV + 3 * g
                    second(jq, i * 6, between=(lambda: weights_exp(0)) if g else None)
                    first(jq + 1, i * 6)
                    second(jq + 1, i * 6)
                    first(jq + 2, i * 6)
                    ka = A_QKV + 3 * g + 1
                    act.wait_ge(parts_used, used(jq + 1, i * 6))
                    for b in range(2):
                        nc.scalar.copy(kT[:, 2 * b:2 * b + 2, :], banks[2 * (ka % 2) + b][:, :].rearrange(
                            "p (h s) -> p h s", h=2)).then_inc(acc_evac[ka % 2], 1)
                    second(jq + 2, i * 6, between=lambda: softplus_log(g))
                    first(jq + 3, i * 6)
                    va = A_QKV + 3 * g + 2
                    act.wait_ge(parts_used, used(jq + 2, i * 6))
                    for m in range(MT):
                        nc.scalar.copy(V[:, m, :], banks[2 * (va % 2) + m][:, :]).then_inc(acc_evac[va % 2], 1)
                weights_exp(1)
            wait_aux_evac(act, X["sb"] + 47)
            for n in range(4):
                nc.scalar.copy(Ah[:, n * 1024:n * 1024 + 1024], oraw[:, n * 1024:n * 1024 + 1024]).then_inc(a_hi, 1)
            residual_jobs(J_WO, A_WO)
            root(1)
            take_transposed(X["norm1"], 1)

            act.sem_inc(h_ready, 2)
            for half, (j1, j2, a1, a2) in enumerate(((J_W1, J_W2, A_W1, A_W2), (J_W1B, J_W2B, A_W1B, A_W2B))):
                with act.Fori(0, 4) as i:
                    for n in range(2):
                        second(j1 + n, i * 2)
                        first(j1 + n + 1, i * 2)
                        act.wait_ge(parts_used, used(j1 + n, i * 2))
                        act.wait_ge(h_ready, 8 * half + n + 1 + i * 2)
                        for b in range(2):
                            nc.scalar.activation(tmp[:, n * 1024 + b * 512:n * 1024 + b * 512 + 512],
                                                 banks[2 * n + b][:, :], ACT.Relu).then_inc(acc_evac[n], 1)
                        act.wait_ge(h_squared, 8 * half + n + 1 + i * 2)
                        nc.scalar.copy(hTh[:, bass.ds(i * 2048 + n * 1024, 1024)], tmp[:, n * 1024:n * 1024 + 1024]
                                       ).then_inc(h_hi, 1)
                with act.Fori(0, 2) as i:
                    for n in range(2):
                        for kq in range(2):
                            second(j2 + 2 * n + kq, i * 4)
                            first(j2 + 2 * n + kq + 1, i * 4)
                        if half:
                            job_squares(a2 + n, n, i)
            root(2)
            act.wait_ge(x2_ready, 2)
            all_squares()
            root(3)
            take_transposed(X["norm2"], 2)

            for n in range(8):
                second(J_WIN + n, width=512 if n < 7 else WIN_REST)
                if n < 7:
                    first(J_WIN + n + 1, width=512 if n < 6 else WIN_REST)
                act.wait_ge(parts_used, used(J_WIN + n))
                ps = [banks[2 * (n % 2) + m] for m in range(MT)]
                for m in range(MT):
                    if n < 2:
                        nc.scalar.copy(U[:, m, n * 512:n * 512 + 512], ps[m][:, :]).then_inc(acc_evac[n % 2], 1)
                    elif n < 4:
                        for l in range(2):
                            q_raw = nc.scalar.copy(qn[:, m, n - 2, :, l, :], ps[m][:, l * 256:l * 256 + 256].rearrange(
                                "p (r d) -> p r d", r=R))
                        q_raw.then_inc(acc_evac[n % 2], 1)
                    elif n == 4:
                        nc.scalar.copy(kvc[:, m, :].rearrange("p (g v d) -> p v g d", g=G, v=2),
                                       ps[m][:, :].rearrange("p (v g d) -> p v g d", v=2, g=G)).then_inc(acc_evac[n % 2], 1)
                    elif n < 7:
                        nc.scalar.copy(kn[:, n - 5, m, :], ps[m][:, 0:256])
                        nc.scalar.copy(vn[:, n - 5, m, :], ps[m][:, 256:512]).then_inc(acc_evac[n % 2], 1)
                    else:
                        nc.scalar.activation(gates[:, m * WIN_REST:(m + 1) * WIN_REST], ps[m][:, 0:WIN_REST],
                                             ACT.Sigmoid).then_inc(acc_evac[n % 2], 1)
            act.wait_ge(head_ms, 1)
            nc.scalar.activation(nrm[:, 64:96], nrm[:, 0:32], ACT.Sqrt).then_inc(head_rt, 1)
            act.wait_ge(head_ms, 2)
            nc.scalar.activation(nrm[:, 96:112], nrm[:, 32:48], ACT.Sqrt).then_inc(head_rt, 1)
            act.wait_ge(small_landed, 16 * 8)
            for c in range(8):
                k = X["pool"] + c // 2
                act.wait_ge(aux_done, k + 1)
                nc.scalar.activation(Ah_v[:, c, :], aux(k)[:, (c % 2) * S:(c % 2 + 1) * S], ACT.Copy,
                                     scale=psc[:, c:c + 1]).then_inc(a_hi, 1)
            for v in range(2):
                k = X["hid"] + v
                act.wait_ge(aux_done, k + 1)
                for h in range(2):
                    g1 = nc.scalar.activation(hc[:, v, h, :], aux(k)[:, h * P:h * P + P], ACT.Gelu,
                                              bias=b1c[:, 2 * v + h:2 * v + h + 1])
                g1.then_inc(aux_evac[k % 4], 1)
            act.wait_ge(head_ms, 3)
            nc.scalar.activation(nrm[:, 112:113], nrm[:, 48:49], ACT.Sqrt).then_inc(head_rt, 1)
            act.wait_ge(cmp_shift, 1)
            nc.scalar.activation(cex3, csc3, ACT.Exp).then_inc(cmp_exp, 1)
            def take_turned(u):
                q = u % 2
                k = att_use(u, 1)
                act.wait_ge(aux_done, k + 1)
                if u >= 2:
                    act.wait_ge(pv_done, u - 1)
                n = 2 * (q + 1)
                nc.scalar.copy(pA[q][:, 0:n, :], aux(k)[:, 0:n * P].rearrange("p (n s) -> p n s", n=n)
                               ).then_inc(aux_evac[k % 4], 1)

            def out_hi(hp):
                act.wait_ge(pv_done, 4 * hp + 4)
                nc.scalar.copy(Ah_v[:, 8 + hp, :], banks[hp % 2][:, 0:S]).then_inc(a_hi, 1)

            for u in range(32):
                w = P * (u % 2 + 1)
                act.wait_ge(s_ready, u + 1)
                for b in range(2):
                    e = nc.scalar.activation(eA[u % 2][:, b, 0:w], sA[u % 2][:, b, 0:w], ACT.Exp,
                                             bias=nrm[:, 4 * (u % 2) + b:4 * (u % 2) + b + 1],
                                             accum_out=nrm[:, 4 * (u % 2) + 2 + b:4 * (u % 2) + 3 + b])
                    e.then_inc(e_ready, 1)
                if u >= 1:
                    take_turned(u - 1)
                if u >= 5 and (u - 5) % 4 == 0:
                    out_hi((u - 5) // 4)
                if u in (15, 19, 23, 27):
                    conv(J_WOUT, (u - 15) // 4)
            take_turned(31)
            out_hi(7)
            act.wait_ge(pv_evac, 8)
            act.dma_start(gbc[:, :], a["ffn_norm_w"].rearrange("(o d) -> o d", o=1).broadcast_to((P, D))
                          ).then_inc(gbc_landed, 16)
            residual_jobs(J_WOUT, A_WOUT)
            root(4)
            take_transposed(X["norm3"], 3)

            for j in range(4):
                n = j % 2
                second(J_WQ + j)
                if j < 3:
                    first(J_WQ + j + 1)
                act.wait_ge(parts_used, used(J_WQ + j))
                for b in range(2):
                    nc.scalar.copy(qp[n][:, 2 * b:2 * b + 2, :], banks[2 * n + b][:, :].rearrange(
                        "p (f s) -> p f s", f=2)).then_inc(acc_evac[n], 1)
                if n == 1:
                    for u in range(4):
                        k = X["psc"] + 2 * (j - 1) + u
                        f0 = 4 * (j - 1 + u // 2)
                        act.wait_ge(aux_done, k + 1)
                        nc.scalar.copy(scm[u % 2][:, f0:f0 + 4, :], aux(k)[:, :].rearrange("p (h k) -> p h k", h=4)
                                       ).then_inc(aux_evac[k % 4], 1)
            for m in range(MT):
                act.wait_ge(best_shift, m + 1)
                nc.scalar.activation(bv, bv, ACT.Exp).then_inc(best_exp, 1)
            for m in range(MT):
                per = SLOTS // (GROUPS * EG)
                with act.Fori(0, per) as i:
                    for g in range(GROUPS):
                        act.wait_ge(dots_done[g], EG * (m * per + 1) + i * EG)
                        nc.scalar.activation(hgel[:, g * EG:(g + 1) * EG], hcur[:, g * EG:(g + 1) * EG], ACT.Gelu
                                             ).then_inc(gelu_done[g], 1)
                act.wait_ge(peer_added, m + 1)
                for n in range(NT):
                    nc.scalar.activation(tm[:, m, n * 512:n * 512 + 512], xr[:, m, n * 512:n * 512 + 512], ACT.Square,
                                         accum_out=ss[:, m * NT + n:m * NT + n + 1]).then_inc(sq_done, 1)
            root(5)
            first(J_GATE)
            take_transposed(X["norm4"], 4)
            for n in range(NT):
                second(J_GATE + n)
                if n < 3:
                    first(J_GATE + n + 1)
                act.wait_ge(parts_used, used(J_GATE + n))
                if n >= 2:
                    act.wait_ge(out_ready, 2 * (n - 1))
                for m in range(MT):
                    nc.scalar.activation(sg[n % 2][m], banks[2 * (n % 2) + m][:, :], ACT.Sigmoid
                                         ).then_inc(acc_evac[n % 2], 1)

        @block.vector
        def _(dve):
            links = [0]

            def link(ins):
                links[0] += 1
                ins.then_inc(dve_link, 1)
                dve.wait_ge(dve_link, links[0])

            V_ = nc.vector

            def rms(n):
                dve.wait_ge(sq_done, 8 * (n + 1))
                link(V_.tensor_reduce(ms[:, :], v3(ss, 0, MT, NT), AX_X, ALU.add))
                V_.tensor_scalar(ms[:, :], ms[:, :], 1.0 / D, EPS, ALU.mult, ALU.add).then_inc(ms_ready, 1)
                dve.wait_ge(rt_ready, n + 1)
                link(V_.reciprocal(rstd[:, :], rt[:, :]))

            def scale_rows():
                for m in range(MT):
                    V_.tensor_scalar(tm[:, m, :], xr[:, m, :], rstd[:, m:m + 1], None, ALU.mult).then_inc(scaled, 1)

            def take_transposed(k0, gain, h0):
                for c in range(KC):
                    if c % 2 == 0:
                        dve.wait_ge(a_hi, h0 + c + 2)
                    lo = V_.scalar_tensor_tensor(Al_v[:, c, :], aux(k0 + c // 2)[:, (c % 2) * S:(c % 2 + 1) * S],
                                                 gT[:, 16 * gain + c:16 * gain + c + 1], Ahf[:, c, :],
                                                 ALU.mult, ALU.subtract)
                    if c % 2:
                        lo.then_inc(aux_evac[(k0 + c // 2) % 4], 1)

            def conv(j, hq, d=0, width=512):
                split_jobs = j - (j > J_CMP)
                dve.wait_ge(hi_done, 8 * split_jobs + hq + 1 + d * 8)
                V_.tensor_tensor(wlv[hq % 4][:, :, 0:width], raw_half[hq][:, :, 0:width], whf[hq % 4][:, :, 0:width],
                                 ALU.subtract).then_inc(split_done, 1)

            def first(j, d=0, width=512):
                for hq in range(4):
                    conv(j, hq, d, width)

            def second(j, d=0, width=512, between=None):
                conv(j, 4, d, width)
                if between is not None:
                    between()
                for hq in range(5, 8):
                    conv(j, hq, d, width)

            def add_tile(j, n, d, i):
                dve.wait_ge(parts_used, used(j, d))
                for m in range(MT):
                    cols = bass.ds(i * 1024 + n * 512, 512)
                    V_.tensor_tensor(xr[:, m, cols], xr[:, m, cols], banks[2 * n + m][:, :], ALU.add
                                     ).then_inc(acc_evac[n], 1)

            def residual_jobs(j0):
                with dve.Fori(0, 2) as i:
                    for n in range(2):
                        second(j0 + n, i * 2)
                        first(j0 + n + 1, i * 2)
                        add_tile(j0 + n, n, i * 2, i)

            V_.memset(relb[32:33, :], NEG).then_inc(mask_row, 1)
            dve.wait_ge(aux_done, X["gain"] + 1)
            V_.tensor_copy(gT[:, :], aux(X["gain"])[:, 0:80]).then_inc(aux_evac[X["gain"] % 4], 1)
            rms(0)
            scale_rows()
            first(J_QKV)
            take_transposed(X["norm0"], 0, H_NORM0)

            with dve.Fori(0, 2) as i:
                def log_weights(g):
                    for h in range(4):
                        k = X["sb"] + 12 * g + 4 + h
                        dve.wait_ge(aux_done, k + 1 + i * 24)
                        V_.tensor_tensor(at[:, h, :], zm[:, h, :], aux(k)[:, 0:TRI_W], ALU.subtract
                                         ).then_inc(aux_evac[k % 4], 1)

                def take_outputs(g):
                    for h in range(4):
                        k = X["sb"] + 12 * g + 8 + h
                        dve.wait_ge(aux_done, k + 1 + i * 24)
                        V_.tensor_copy(oraw[:, bass.ds(i * 2048 + (g * 1024 + h * S), S)], aux(k)[:, 0:S]
                                       ).then_inc(aux_evac[k % 4], 1)

                def masked_logits(g):
                    for h in range(4):
                        k = X["sb"] + 12 * g + h
                        dve.wait_ge(aux_done, k + 1 + i * 24)
                        V_.tensor_tensor(zm[:, h, :], aux(k)[:, 0:TRI_W], neg, ALU.add).then_inc(aux_evac[k % 4], 1)

                for g in range(2):
                    jq = J_QKV + 3 * g
                    ps = 3 * g % 2
                    second(jq, i * 6, between=(lambda: log_weights(0)) if g else None)
                    first(jq + 1, i * 6)
                    dve.wait_ge(parts_used, used(jq, i * 6))
                    for b in range(2):
                        V_.tensor_scalar(qT[:, 2 * b:2 * b + 2, :], banks[2 * ps + b][:, :].rearrange(
                            "p (h s) -> p h s", h=2), SB_SCALE, None, ALU.mult).then_inc(acc_evac[ps], 1)
                    second(jq + 1, i * 6, between=(lambda: take_outputs(0)) if g else None)
                    first(jq + 2, i * 6)
                    second(jq + 2, i * 6, between=lambda: masked_logits(g))
                    dve.wait_ge(soft_ready, 3 * g + 3 + i * 6)
                    V_.scalar_tensor_tensor(sp, zm, 0.0, ee, ALU.max, ALU.add).then_inc(sp_ready, 1)
                    first(jq + 3, i * 6)
                log_weights(1)
                take_outputs(1)
            for n in range(4):
                dve.wait_ge(a_hi, H_O + n + 1)
                V_.tensor_tensor(Al[:, n * 1024:n * 1024 + 1024], oraw[:, n * 1024:n * 1024 + 1024],
                                 Ah[:, n * 1024:n * 1024 + 1024].bitcast(F32), ALU.subtract).then_inc(a_lo, 1)
            residual_jobs(J_WO)
            rms(1)
            scale_rows()
            take_transposed(X["norm1"], 1, H_NORM1)

            for half, (j1, j2, a1) in enumerate(((J_W1, J_W2, A_W1), (J_W1B, J_W2B, A_W1B))):
                with dve.Fori(0, 4) as i:
                    for n in range(2):
                        second(j1 + n, i * 2)
                        first(j1 + n + 1, i * 2)
                        wait_acc_evac(dve, a1 + n, i * 2)
                        h = tmp[:, n * 1024:n * 1024 + 1024]
                        V_.tensor_tensor(h, h, h, ALU.mult).then_inc(h_squared, 1)
                        dve.wait_ge(h_hi, 8 * half + n + 1 + i * 2)
                        cols = bass.ds(i * 2048 + n * 1024, 1024)
                        V_.tensor_tensor(hTl[:, cols], h, hThf[:, cols], ALU.subtract).then_inc(h_ready, 1)
                with dve.Fori(0, 2) as i:
                    for n in range(2):
                        for kq in range(2):
                            second(j2 + 2 * n + kq, i * 4)
                            first(j2 + 2 * n + kq + 1, i * 4)
                        add_tile(j2 + 2 * n + 1, n, i * 4, i)
            rms(2)
            dve.wait_ge(gbc_landed, 16)
            for m in range(MT):
                V_.scalar_tensor_tensor(xr[:, m, :], xr[:, m, :], rstd[:, m:m + 1], gbc[:, :], ALU.mult, ALU.mult
                                        ).then_inc(x2_ready, 1)
            rms(3)
            dve.wait_ge(x2_ready, 2)
            scale_rows()
            take_transposed(X["norm2"], 2, H_NORM2)

            def take_flips(piece):
                for f in range(3 * piece, 3 * piece + 3):
                    k = X["flip"] + f
                    dve.wait_ge(aux_done, k + 1)
                    V_.tensor_copy(big[:, 10240 + f * 512:10240 + f * 512 + 512], aux(k)[:, :]
                                   ).then_inc(aux_evac[k % 4], 1)

            for n in range(8):
                second(J_WIN + n, width=512 if n < 7 else WIN_REST)
                if n < 7:
                    first(J_WIN + n + 1, width=512 if n < 6 else WIN_REST)
                if n == 0:
                    dve.wait_ge(aux_done, X["line"] + 1)
                    V_.tensor_copy(gbc[0:16, 0:512], aux(X["line"])[0:16, :]).then_inc(aux_evac[X["line"] % 4], 1)
                if n == 2 or n == 4:
                    take_flips(n - 2)
                    take_flips(n - 1)

            def head_norm(t3, heads, at_, sq, n):
                link(V_.tensor_tensor(sq, t3, t3, ALU.mult))
                link(V_.tensor_reduce(nrm[:, at_:at_ + heads], sq, AX_X, ALU.add))
                V_.tensor_scalar(nrm[:, at_:at_ + heads], nrm[:, at_:at_ + heads], 1.0 / DK, EPS, ALU.mult, ALU.add
                                 ).then_inc(head_ms, 1)
                dve.wait_ge(head_rt, n + 1)
                link(V_.reciprocal(nrm[:, at_ + 128:at_ + 128 + heads], nrm[:, at_ + 64:at_ + 64 + heads]))
                return nrm[:, at_ + 128:at_ + 128 + heads].unsqueeze(2)

            wait_acc_evac(dve, A_WIN + 3)
            wait_acc_evac(dve, A_WIN + 2)
            r = head_norm(qn3, 32, 0, v3(tmp, 0, 32, DK), 0)
            link(V_.tensor_tensor(qn3, qn3, r.broadcast_to((P, 32, DK)), ALU.mult))
            V_.scalar_tensor_tensor(qn3, qn3, DK ** -0.5, qnw[:, :].unsqueeze(1).broadcast_to((P, 32, DK)),
                                    ALU.mult, ALU.mult).then_inc(qk_norm, 1)
            wait_acc_evac(dve, A_WIN + 5)
            wait_acc_evac(dve, A_WIN + 6)
            r = head_norm(kn3, 16, 32, v3(tmp, 2048, 16, DK), 1)
            link(V_.tensor_tensor(kn3, kn3, r.broadcast_to((P, 16, DK)), ALU.mult))
            V_.tensor_tensor(kn3, kn3, knw[:, :].unsqueeze(1).broadcast_to((P, 16, DK)), ALU.mult
                             ).then_inc(qk_norm, 1)
            wait_acc_evac(dve, A_WIN + 7)
            for k0, n, dst in ((X["qt"], 4, 4096), (X["kt"], 2, 9216)):
                for u in range(n):
                    k = k0 + u
                    dve.wait_ge(aux_done, k + 1)
                    V_.tensor_copy(big[:, dst + u * 512:dst + u * 512 + 512], aux(k)[:, :]).then_inc(aux_evac[k % 4], 1)
            for u in range(2):
                k = X["ct"] + u
                dve.wait_ge(aux_done, k + 1)
                V_.tensor_copy(cT[:, 2 * u:2 * u + 2, :], aux(k)[:, :].rearrange("p (g s) -> p g s", g=2)
                               ).then_inc(aux_evac[k % 4], 1)
            wait_aux_evac(dve, X["ct"] + 1)
            for g in range(G):
                for half in range(2):
                    src = cT[:, g, 16 * half:16 * half + 16 * NCMP].rearrange("p (c l) -> p c l", l=16)
                    last = V_.tensor_tensor(flat[:, 16 * half:16 * half + 16, g, 0:NCMP].rearrange("p l c -> p c l"), src,
                                            posT[:, 16 * half:16 * half + 16].unsqueeze(1).broadcast_to((P, NCMP, 16)),
                                            ALU.add)
            last.then_inc(flat_ready, 1)
            for u in range(4):
                k = X["mixed"] + u
                dve.wait_ge(aux_done, k + 1)
                V_.tensor_copy(mixT[:, 2 * u:2 * u + 2, :], aux(k)[:, :].rearrange("p (c s) -> p c s", c=2)
                               ).then_inc(aux_evac[k % 4], 1)
            for g in range(4):
                k = X["pool"] + g
                dve.wait_ge(aux_done, k + 1)
                dve.wait_ge(a_hi, H_MIX + 2 * g + 2)
                for c in range(2 * g, 2 * g + 2):
                    lo = V_.scalar_tensor_tensor(Al_v[:, c, :], aux(k)[:, (c % 2) * S:(c % 2 + 1) * S], psc[:, c:c + 1],
                                                 Ahf[:, c, :], ALU.mult, ALU.subtract)
                lo.then_inc(aux_evac[k % 4], 1)
            k = X["cmp"]
            dve.wait_ge(pads_ready, 2)
            dve.wait_ge(aux_done, k + 1)
            for g in range(G):
                V_.tensor_copy(Vcm[32 * g:32 * g + NCMP, g, :], aux(k)[32 * g:32 * g + NCMP, DK:2 * DK])
            link(V_.tensor_copy(kc2[:, 0, :], aux(k)[:, 0:DK]))
            link(V_.tensor_tensor(kc2[:, 1, :], kc2[:, 0, :], kc2[:, 0, :], ALU.mult))
            link(V_.tensor_reduce(nrm[:, 48:49], kc2[:, 1, :], AX_X, ALU.add))
            V_.tensor_scalar(nrm[:, 48:49], nrm[:, 48:49], 1.0 / DK, EPS, ALU.mult, ALU.add).then_inc(head_ms, 1)
            dve.wait_ge(head_rt, 3)
            link(V_.reciprocal(nrm[:, 176:177], nrm[:, 112:113]))
            link(V_.scalar_tensor_tensor(kc2[:, 0, :], kc2[:, 0, :], nrm[:, 176:177], knw[:, :], ALU.mult, ALU.mult))
            V_.tensor_copy(kc2[:, 1, :], kc2[:, 0, :]).then_inc(aux_evac[k % 4], 1)
            k = X["kct"]
            dve.wait_ge(aux_done, k + 1)
            V_.tensor_copy(kcT, aux(k)[:, 0:P]).then_inc(aux_evac[k % 4], 1)
            V_.memset(csc3[:, :, NCMP:CPAD], NEG)
            for l in range(2):
                k = X["csc"] + l
                dve.wait_ge(aux_done, k + 1)
                for q in range(MT):
                    off = 255 - P * q - (P - 1) + CMP_L - 1
                    for j in range(2):
                        bias = TB[:, (2 * j + l) * R:(2 * j + l) * R + R, off:off + CMP_S * (NCMP - 1) + 1:CMP_S]
                        pv = aux(k)[:, q * P:(q + 1) * P].rearrange("p (r j c) -> p r j c", r=R, j=2)
                        last = V_.tensor_tensor(csc[:, l, q, :, j, 0:NCMP], pv[:, :, j, 0:NCMP], bias, ALU.add)
                last.then_inc(aux_evac[k % 4], 1)
            wait_aux_evac(dve, X["csc"] + 1)
            link(V_.tensor_reduce(nrm[:, 0:32], csc3, AX_X, ALU.max))
            link(V_.tensor_scalar(Pc3[:, 0:4, :].rearrange("p a (b c) -> p (a b) c", c=CPAD), csc3, NEG / 2, None,
                                  ALU.is_gt))
            V_.tensor_tensor(csc3, csc3, nrm[:, 0:32].unsqueeze(2).broadcast_to((P, 32, CPAD)), ALU.subtract
                             ).then_inc(cmp_shift, 1)
            dve.wait_ge(cmp_exp, 1)
            mask = Pc3[:, 0:4, :].rearrange("p a (b c) -> p (a b) c", c=CPAD)
            link(V_.tensor_tensor(cex3, cex3, mask, ALU.mult))
            link(V_.tensor_reduce(nrm[:, 32:64], cex3, AX_X, ALU.add))
            link(V_.tensor_scalar(nrm[:, 32:64], nrm[:, 32:64], 1e-30, None, ALU.max))
            link(V_.reciprocal(nrm[:, 64:96], nrm[:, 32:64]))
            rc = nrm[:, 64:96].rearrange("p (l q r j) -> p l q r j", l=2, q=MT, r=R)
            gv = gates[:, :].rearrange("p (m j l r b) -> p m j l r b", m=MT, j=2, l=2, r=R)
            for l in range(2):
                for q in range(MT):
                    last = V_.tensor_tensor(rc[:, l, q, :, :].rearrange("p r j -> p j r"),
                                            rc[:, l, q, :, :].rearrange("p r j -> p j r"),
                                            gv[:, q, :, l, :, 0], ALU.mult)
            link(last)
            link(V_.memset(big[:, 1024:2048], 0.0))
            cexv = cex3[:, :, :].rearrange("p (l q r j) c -> p l q r j c", l=2, q=MT, r=R)
            for l in range(2):
                for q in range(MT):
                    for j in range(2):
                        last = V_.tensor_tensor(Pc[:, q, :, 2 * j + l, 0:CPAD], cexv[:, l, q, :, j, :],
                                                rc[:, l, q, :, j].unsqueeze(2).broadcast_to((P, R, CPAD)), ALU.mult)
            last.then_inc(pc_ready, 1)
            for u in range(2):
                k = X["pct"] + u
                dve.wait_ge(aux_done, k + 1)
                V_.tensor_copy(PcT[:, 4 * u:4 * u + 4, :], aux(k)[:, :].rearrange("p (n s) -> p n s", n=4)
                               ).then_inc(aux_evac[k % 4], 1)

            def logits(u):
                h, q = u // 2, u % 2
                w = P * (q + 1)
                k = att_use(u, 0)
                dve.wait_ge(aux_done, k + 1)
                if u >= 2:
                    dve.wait_ge(e_ready, 2 * (u - 1))
                (V_.tensor_tensor(sA[q][:, :, 0:w], aux(k)[:, :].rearrange(
                    "p (b s) -> p b s", b=2)[:, :, 0:w], TB[:, h, S - w:S].unsqueeze(1).broadcast_to((P, 2, w)), ALU.add)
                 ).then_inc(aux_evac[k % 4], 1)
                wait_aux_evac(dve, k)
                link(V_.tensor_reduce(nrm[:, 4 * q:4 * q + 2], sA[q][:, :, 0:w], AX_X, ALU.max))
                V_.tensor_scalar(nrm[:, 4 * q:4 * q + 2], nrm[:, 4 * q:4 * q + 2], -1.0, None, ALU.mult
                                 ).then_inc(s_ready, 1)

            def weights(u):
                h, q = u // 2, u % 2
                w = P * (q + 1)
                dve.wait_ge(e_ready, 2 * (u + 1))
                c = nrm[:, 16 + 4 * q:18 + 4 * q]
                link(V_.reciprocal(c, nrm[:, 4 * q + 2:4 * q + 4]))
                g0 = q * WIN_REST + h * 3
                link(V_.tensor_tensor(c, c, gates[:, g0 + 1:g0 + 3], ALU.mult))
                V_.tensor_tensor(eA[q][:, :, 0:w], eA[q][:, :, 0:w], c.unsqueeze(2).broadcast_to((P, 2, w)), ALU.mult
                                 ).then_inc(p_ready, 1)

            def take_out(hp):
                dve.wait_ge(a_hi, H_MIX + 8 + hp + 1)
                V_.tensor_tensor(Al_v[:, 8 + hp, :], banks[hp % 2][:, 0:S], Ahf[:, 8 + hp, :], ALU.subtract
                                 ).then_inc(pv_evac, 1)

            for u in range(33):
                if u < 32:
                    logits(u)
                if u >= 1:
                    weights(u - 1)
                    if u >= 5 and (u - 5) % 4 == 0:
                        take_out((u - 5) // 4)
                if u in (15, 19, 23, 27):
                    conv(J_WOUT, (u - 15) // 4)
            take_out(7)

            residual_jobs(J_WOUT)
            for u in range(4):
                k = X["skt"] + u
                dve.wait_ge(aux_done, k + 1)
                V_.tensor_copy(skT[:, 4 * u:4 * u + 4, :], aux(k)[:, :].rearrange("p (n s) -> p n s", n=4)
                               ).then_inc(aux_evac[k % 4], 1)
            rms(4)
            scale_rows()
            take_transposed(X["norm3"], 3, H_NORM3)
            dve.wait_ge(gbc_landed, 32)
            for m in range(MT):
                V_.tensor_tensor(xn[:, m, :], tm[:, m, :], gbc[:, :], ALU.mult).then_inc(xn_ready, 1)

            def best_keys(m, f0):
                fs = range(f0, f0 + 4)
                for f in fs:
                    last = V_.max(topv[m][:, f, 0:8], scm[m][:, f, :])
                link(last)
                for f in fs:
                    V_.max_index(topi[m][:, f, 0:8], topv[m][:, f, 0:8], scm[m][:, f, :])
                for f in fs:
                    last = V_.match_replace(scw[:, f, :], topv[m][:, f, 0:8], scm[m][:, f, :], -3e38)
                link(last)
                for f in fs:
                    last = V_.max(topv[m][:, f, 8:16], scw[:, f, :])
                link(last)
                for f in fs:
                    last = V_.max_index(topi[m][:, f, 8:16], topv[m][:, f, 8:16], scw[:, f, :])
                link(last)

            for j in range(4):
                for hq in range(4, 8):
                    conv(J_WQ + j, hq)
                    if j >= 2 and hq == 5:
                        wait_aux_evac(dve, X["psc"] + 2 * (j - 2))
                        best_keys(0, 4 * (j - 2))
                if j < 3:
                    for hq in range(4):
                        conv(J_WQ + j + 1, hq)
                        if j == 2 and hq == 0:
                            wait_aux_evac(dve, X["psc"] + 1)
                            best_keys(1, 0)

            wait_aux_evac(dve, X["psc"] + 3)
            best_keys(1, 4)
            for m in range(MT):
                for n in range(2):
                    wait_aux_evac(dve, X["psc"] + 4 + 2 * n + m)
                    best_keys(m, 8 + 4 * n)
                link(V_.tensor_copy(topf, topi[m]))
                t4 = topv[m][:, :, :].rearrange("p (h b) k -> p h b k", b=2)
                for h in range(PH):
                    last = V_.tensor_tensor(cand[:, h, :].rearrange("p (i j) -> p i j", i=TOPK),
                                            t4[:, h, 0, :].unsqueeze(2).broadcast_to((P, TOPK, TOPK)),
                                            t4[:, h, 1, :].unsqueeze(1).broadcast_to((P, TOPK, TOPK)), ALU.add)
                link(last)
                for h in range(PH):
                    last = V_.max(bv[:, h, 0:8], cand[:, h, :])
                link(last)
                for h in range(PH):
                    V_.max_index(bp[:, h, 0:8], bv[:, h, 0:8], cand[:, h, :])
                for h in range(PH):
                    last = V_.match_replace(candw[:, h, :], bv[:, h, 0:8], cand[:, h, :], -3e38)
                link(last)
                for h in range(PH):
                    last = V_.max(bv[:, h, 8:16], candw[:, h, :])
                link(last)
                for h in range(PH):
                    last = V_.max_index(bp[:, h, 8:16], bv[:, h, 8:16], candw[:, h, :])
                link(last)
                f4 = topf[:, :, :].rearrange("p (h b) k -> p h b k", b=2)
                for part, op, arg, res in ((0, ALU.logical_shift_right, 4, i1), (1, ALU.bitwise_and, 15, i2)):
                    link(V_.tensor_scalar(pq, bp, arg, None, op))
                    link(V_.tensor_copy(pf, pq[:, :, :].rearrange("p h k -> p (h k)")))
                    link(V_.tensor_tensor(oh, pf.unsqueeze(2).broadcast_to((P, SLOTS, TOPK)),
                                          iota16.unsqueeze(1).broadcast_to((P, SLOTS, TOPK)), ALU.is_equal))
                    oh4 = oh[:, :, :].rearrange("p (h k) t -> p h k t", h=PH)
                    for h in range(PH):
                        last = V_.tensor_tensor(oh4[:, h], oh4[:, h], f4[:, h, part, :].unsqueeze(1).broadcast_to(
                            (P, TOPK, TOPK)), ALU.mult)
                    link(last)
                    link(V_.tensor_reduce(res, oh, AX_X, ALU.add))
                V_.scalar_tensor_tensor(idx[:, m * SLOTS:(m + 1) * SLOTS], i1, float(NK), i2, ALU.mult, ALU.add
                                        ).then_inc(idx_ready, 1)
                link(V_.tensor_copy(bs[:, 0:PH], bv[:, :, 0]))
                V_.tensor_tensor(bv, bv, bs[:, 0:PH].unsqueeze(2).broadcast_to((P, PH, TOPK)), ALU.subtract
                                 ).then_inc(best_shift, 1)
                dve.wait_ge(best_exp, m + 1)
                link(V_.tensor_reduce(bs[:, 8:16], bv, AX_X, ALU.add))
                link(V_.reciprocal(bs[:, 16:24], bs[:, 8:16]))
                V_.tensor_tensor(gts[:, m * SLOTS:(m + 1) * SLOTS].rearrange("p (h k) -> p h k", h=PH), bv,
                                 bs[:, 16:24].unsqueeze(2).broadcast_to((P, PH, TOPK)), ALU.mult).then_inc(routed, 1)
            dve.wait_ge(acc_zero, 1)
            dve.wait_ge(routed, MT)
            dve.wait_ge(xn_ready, MT)

            per = SLOTS // (GROUPS * EG)
            for m in range(MT):
                with dve.Fori(0, per) as i:
                    def dots(g):
                        dve.wait_ge(u_landed[g], 16 * EG * (m * per + 1) + i * (16 * EG))
                        for b in range(EG):
                            V_.tensor_tensor_reduce(out=ubuf[g][b], in0=ubuf[g][b], in1=xn[:, m, :], scale=1.0,
                                                    scalar=0.0, op0=ALU.mult, op1=ALU.add,
                                                    accum_out=hcur[:, g * EG + b:g * EG + b + 1]
                                                    ).then_inc(dots_done[g], 1)

                    def adds(g):
                        dve.wait_ge(gelu_done[g], m * per + 1 + i)
                        V_.tensor_tensor(wcur[:, g * EG:(g + 1) * EG], hgel[:, g * EG:(g + 1) * EG],
                                         gts[:, bass.ds(i * (GROUPS * EG) + (m * SLOTS + g * EG), EG)], ALU.mult
                                         ).then_inc(w_done, 1)
                        dve.wait_ge(w_done, GROUPS * m * per + g + 1 + i * GROUPS)
                        dve.wait_ge(v_landed[g], 16 * EG * (m * per + 1) + i * (16 * EG))
                        for b in range(EG):
                            V_.scalar_tensor_tensor(accx[:, m, :], vbuf[g][b], wcur[:, g * EG + b:g * EG + b + 1],
                                                    accx[:, m, :], ALU.mult, ALU.add).then_inc(v_done[g], 1)
                            dve.wait_ge(v_done[g], EG * m * per + EG + b + 1 + i * EG)

                    dots(0)
                    for g in range(1, GROUPS):
                        dots(g)
                        adds(g - 1)
                    adds(GROUPS - 1)
                V_.tensor_tensor(xr[:, m, :], xr[:, m, :], accx[:, m, :], ALU.add).then_inc(peer_added, 1)
            rms(5)
            scale_rows()
            first(J_GATE)
            k = X["pt"]
            dve.wait_ge(aux_done, k + 1)
            V_.tensor_copy(pT, aux(k)[:, :].rearrange("p (c s) -> p c s", c=2)).then_inc(aux_evac[k % 4], 1)
            take_transposed(X["norm4"], 4, H_NORM4)
            for n in range(NT):
                second(J_GATE + n)
                if n < 3:
                    first(J_GATE + n + 1)
                wait_acc_evac(dve, A_GATE + n)
                for m in range(MT):
                    s = sg[n % 2][m]
                    k = X["pp"] + 2 * n + m
                    dve.wait_ge(aux_done, k + 1)
                    V_.tensor_tensor(s, s, aux(k)[:, :], ALU.mult).then_inc(aux_evac[k % 4], 1)
                    wait_aux_evac(dve, k)
                    V_.tensor_tensor(xr[:, m, n * 512:n * 512 + 512], xr[:, m, n * 512:n * 512 + 512], s, ALU.add
                                     ).then_inc(out_ready, 1)

        @block.tensor
        def _(pe):
            def acc_free(n, more):
                pe.wait_ge(acc_evac[n % 2], 2 * (n // 2) + 2 + more)

            def rows_job(j, n, x=None, width=512, first=True, last=True, k0=0, jd=0, am=0):
                xh, xl = A_ if x is None else x
                if first:
                    acc_free(n, am)
                for hq in range(8):
                    s = hq % 4
                    pe.wait_ge(split_done, 8 * j + hq + 9 + jd * 8)
                    for c in range(2):
                        kc = k0 + 2 * hq + c
                        for m in range(MT):
                            o = banks[2 * (n % 2) + m][:, 0:width]
                            ms_ = slice(m * P, (m + 1) * P)
                            nc.tensor.matmul(o, xh[:, kc, ms_], whv[s][:, c, 0:width],
                                             start=first and hq == 0 and c == 0, stop=False)
                            nc.tensor.matmul(o, xh[:, kc, ms_], wlv[s][:, c, 0:width], start=False, stop=False)
                            mm = nc.tensor.matmul(o, xl[:, kc, ms_], whv[s][:, c, 0:width], start=False,
                                                  stop=last and hq == 7 and c == 1)
                    mm.then_inc(parts_used, 1)

            def cols_job(j, n, jd=0, am=0):
                acc_free(n, am)
                xh, xl = A_
                for hq in range(8):
                    s = hq % 4
                    pe.wait_ge(split_done, 8 * j + hq + 9 + jd * 8)
                    for c in range(2):
                        kc = 2 * hq + c
                        for b in range(4):
                            o = banks[2 * (n % 2) + b // 2][:, (b % 2) * S:(b % 2 + 1) * S]
                            bs_ = slice(b * P, (b + 1) * P)
                            nc.tensor.matmul(o, whv[s][:, c, bs_], xh[:, kc, :], start=kc == 0 and b % 2 == 0,
                                             stop=False, skip_group_check=True)
                            nc.tensor.matmul(o, whv[s][:, c, bs_], xl[:, kc, :], start=False, stop=False,
                                             skip_group_check=True)
                            mm = nc.tensor.matmul(o, wlv[s][:, c, bs_], xh[:, kc, :], start=False, stop=kc == KC - 1,
                                                  skip_group_check=True)
                    mm.then_inc(parts_used, 1)

            def turn(k, pairs):
                for n, (col, src) in enumerate(pairs):
                    mm = nc.tensor.transpose(aux(k)[:, col:col + P], src, ident)
                mm.then_inc(aux_done, 1)

            def turn_stream(k0, norm):
                pe.wait_ge(scaled, 2 * (norm + 1))
                for u in range(8):
                    wait_aux_free(pe, k0 + u)
                    turn(k0 + u, [((2 * c + m) * P, tm[:, m, (2 * u + c) * P:(2 * u + c + 1) * P])
                                  for c in range(2) for m in range(MT)])
                wait_aux_evac(pe, k0 + 7)

            for pair in acc_evac:
                pe.sem_inc(pair, 2)
            pe.sem_inc(parts_used, 4)
            pe.wait_ge(cst_landed, 16)
            pe.wait_ge(gain_landed, 16 * 5)
            nc.tensor.transpose(aux(0)[:, 0:80], tmp[0:80, 0:P], ident[0:80, 0:80]).then_inc(aux_done, 1)
            turn_stream(X["norm0"], 0)

            def sb_scores(g, i):
                wait_acc_evac(pe, A_QKV + 3 * g, i * 6)
                wait_acc_evac(pe, A_QKV + 3 * g + 1, i * 6)
                for h in range(4):
                    k = X["sb"] + 12 * g + h
                    wait_aux_free(pe, k, i * 6)
                    nc.tensor.matmul(aux(k)[:, 0:S], kT[:, h, 0:P], qT[:, h, :], start=True, stop=True)
                    nc.tensor.matmul(aux(k)[:, S:TRI_W], kT[:, h, P:S], qT[:, h, P:S], start=True, stop=True
                                     ).then_inc(aux_done, 1)

            def sb_suffix(g, i):
                pe.wait_ge(sp_ready, g + 1 + i * 2)
                for h in range(4):
                    k = X["sb"] + 12 * g + 4 + h
                    nc.tensor.matmul(aux(k)[:, 0:TRI_W], tri, sp[:, h, :], start=True, stop=False)
                    nc.tensor.matmul(aux(k)[:, P:S], ones, sp[:, h, S:TRI_W], start=False, stop=True
                                     ).then_inc(aux_done, 1)

            def sb_values(g, i):
                pe.wait_ge(at_ready, g + 1 + i * 2)
                wait_acc_evac(pe, A_QKV + 3 * g + 2, i * 6)
                for h in range(4):
                    k = X["sb"] + 12 * g + 8 + h
                    nc.tensor.matmul(aux(k)[:, 0:S], V[:, 0, h * P:(h + 1) * P], at[:, h, 0:S], start=True, stop=False)
                    nc.tensor.matmul(aux(k)[:, P:S], V[:, 1, h * P:(h + 1) * P], at[:, h, S:TRI_W], start=False,
                                     stop=True).then_inc(aux_done, 1)

            with pe.Fori(0, 2) as i:
                for g in range(2):
                    n = 3 * g
                    cols_job(J_QKV + n, A_QKV + n, jd=i * 6, am=i * 6)
                    if g == 1:
                        sb_values(0, i)
                    cols_job(J_QKV + n + 1, A_QKV + n + 1, jd=i * 6, am=i * 6)
                    sb_scores(g, i)
                    rows_job(J_QKV + n + 2, A_QKV + n + 2, jd=i * 6, am=i * 6)
                    sb_suffix(g, i)
                sb_values(1, i)
            pe.wait_ge(a_lo, 4)
            with pe.Fori(0, 2) as i:
                for n in range(2):
                    rows_job(J_WO + n, A_WO + n, jd=i * 2, am=i * 2)
            turn_stream(X["norm1"], 1)

            for half, (j1, j2, a1, a2) in enumerate(((J_W1, J_W2, A_W1, A_W2), (J_W1B, J_W2B, A_W1B, A_W2B))):
                with pe.Fori(0, 4) as i:
                    for n in range(2):
                        cols_job(j1 + n, a1 + n, jd=i * 2, am=i * 2)
                pe.wait_ge(h_ready, 2 + 8 * (half + 1))
                with pe.Fori(0, 2) as i:
                    for n in range(2):
                        for kq in range(2):
                            rows_job(j2 + 2 * n + kq, a2 + n, x=H_, k0=16 * kq, first=kq == 0, last=kq == 1,
                                     jd=i * 4, am=i * 2)
            turn_stream(X["norm2"], 2)

            def flips(piece):
                pe.wait_ge(xp_landed[piece % 2], 16 * (piece // 2 + 1))
                for f in range(3):
                    k = X["flip"] + 3 * piece + f
                    wait_aux_free(pe, k)
                    nc.tensor.matmul(aux(k)[:, :], flip, tmp[:, (piece % 2) * 1536 + f * 512:(piece % 2) * 1536 + f * 512 + 512],
                                     start=True, stop=True).then_inc(aux_done, 1)

            for n in range(8):
                rows_job(J_WIN + n, A_WIN + n, width=512 if n < 7 else WIN_REST)
                if n == 0:
                    pe.wait_ge(mask_row, 1)
                    pe.wait_ge(small_landed, 16 * 8)
                    pe.wait_ge(oh_landed, 16)
                    wait_aux_free(pe, X["line"])
                    nc.tensor.matmul(aux(X["line"])[0:16, :], relb[0:33, :], gbc[0:33, 512:1024], start=True, stop=True
                                     ).then_inc(aux_done, 1)
                if n == 2 or n == 4:
                    flips(n - 2)
                    flips(n - 1)
            pe.wait_ge(qk_norm, 1)
            for u in range(4):
                wait_aux_free(pe, X["qt"] + u)
                turn(X["qt"] + u, [((2 * c + m) * P, big[:, 2048 + m * 1024 + (2 * u + c) * P:2048 + m * 1024 + (2 * u + c + 1) * P])
                                   for c in range(2) for m in range(MT)])
            pe.wait_ge(qk_norm, 2)
            for u in range(2):
                wait_aux_free(pe, X["kt"] + u)
                turn(X["kt"] + u, [((2 * j + m) * P, kn[:, u, m, j * P:(j + 1) * P]) for j in range(2) for m in range(MT)])
            wait_acc_evac(pe, A_WIN + 4)
            for u in range(2):
                wait_aux_free(pe, X["ct"] + u)
                turn(X["ct"] + u, [((2 * c + m) * P, kvc[:, m, (2 * u + c) * P:(2 * u + c + 1) * P])
                                   for c in range(2) for m in range(MT)])
            wait_acc_evac(pe, A_WIN + 1)
            wait_acc_evac(pe, A_WIN + 0)
            pe.wait_ge(misc_landed, 16 * 4)
            band = v3(mrows, 2048, 4, TRI_W)
            poolw = v3(mrows, 0, 8, 256)
            w2c = [v3(cst, P + v * P, 2, DK) for v in range(2)]
            for u in range(4):
                k = X["mixed"] + u
                wait_aux_free(pe, k)
                for c in range(2):
                    cb = 2 * u + c
                    nc.tensor.matmul(aux(k)[:, c * S:(c + 1) * S], U[:, 0, cb * P:(cb + 1) * P], band[:, u, 0:S],
                                     start=True, stop=False)
                    mm = nc.tensor.matmul(aux(k)[:, c * S + P:(c + 1) * S], U[:, 1, cb * P:(cb + 1) * P],
                                          band[:, u, S:TRI_W], start=False, stop=True)
                mm.then_inc(aux_done, 1)
            wait_aux_evac(pe, X["mixed"] + 3)
            for g in range(4):
                k = X["pool"] + g
                wait_aux_free(pe, k)
                for d in range(2):
                    for c in range(2):
                        mm = nc.tensor.matmul(aux(k)[:, d * S:(d + 1) * S], poolw[:, 2 * g + c, d * P:(d + 1) * P],
                                              mixT[:, 2 * g + c, :], start=c == 0, stop=c == 1)
                mm.then_inc(aux_done, 1)
            pe.wait_ge(pads_ready, 1)
            pe.wait_ge(flat_ready, 1)
            for q in range(4):
                pe.wait_ge(w_landed[q], landed(J_CMP, q))
            for v in range(2):
                k = X["hid"] + v
                wait_aux_free(pe, k)
                rows = slice(v * DK, (v + 1) * DK)
                for h in range(2):
                    for l in range(CMP_L):
                        w1 = v3(raw, (l // 8) * 2048, 8, CMP_H)[rows, l % 8, h * P:(h + 1) * P]
                        mm = nc.tensor.matmul(aux(k)[:, h * P:(h + 1) * P], w1, tmp[rows, l * P:(l + 1) * P],
                                              start=l == 0, stop=l == CMP_L - 1)
                mm.then_inc(aux_done, 1)
            wait_aux_evac(pe, X["hid"] + 1)
            pe.sem_inc(split_done, 8)
            pe.sem_inc(parts_used, 8)
            k = X["cmp"]
            wait_aux_free(pe, k)
            for v in range(2):
                for h in range(2):
                    mm = nc.tensor.matmul(aux(k)[:, v * DK:(v + 1) * DK], hc[:, v, h, :], w2c[v][:, h, :],
                                          start=h == 0, stop=h == 1)
            mm.then_inc(aux_done, 1)
            wait_aux_evac(pe, k)
            wait_aux_free(pe, X["kct"])
            turn(X["kct"], [(0, big[:, 3968:4096])])
            wait_aux_evac(pe, X["kct"])
            for l in range(2):
                k = X["csc"] + l
                rows = slice(l * DK, (l + 1) * DK)
                wait_aux_free(pe, k)
                for q in range(MT):
                    for r in range(R):
                        for j in range(2):
                            o = q * P + (2 * r + j) * CPAD
                            mm = nc.tensor.matmul(aux(k)[:, o:o + CPAD], qTa[rows, 4 * j + r, q * P:(q + 1) * P],
                                                  kcT[rows, 32 * (2 * j + l):32 * (2 * j + l) + CPAD], start=True, stop=True)
                mm.then_inc(aux_done, 1)
            pe.wait_ge(pc_ready, 1)
            for q in range(MT):
                k = X["pct"] + q
                wait_aux_free(pe, k)
                turn(k, [(r * P, Pc3[:, 4 * q + r, :]) for r in range(R)])

            def att_logits(u):
                h, q = u // 2, u % 2
                g, r = h // R, h % R
                rows = slice((g % 2) * DK, (g % 2 + 1) * DK)
                w = P * (q + 1)
                k = att_use(u, 0)
                wait_aux_free(pe, k)
                for b in range(2):
                    mm = nc.tensor.matmul(aux(k)[:, b * S:b * S + w], qTa[rows, R * (g // 2) + r, q * P:(q + 1) * P],
                                          kTn[rows, b, g // 2, 0:w], start=True, stop=True)
                mm.then_inc(aux_done, 1)

            def att_turn(u):
                q = u % 2
                k = att_use(u, 1)
                pe.wait_ge(p_ready, u + 1)
                wait_aux_free(pe, k)
                turn(k, [((b * (q + 1) + t) * P, eA[q][:, b, t * P:(t + 1) * P]) for b in range(2) for t in range(q + 1)])

            def att_values(u):
                h, q = u // 2, u % 2
                g, r, hp = h // R, h % R, h // 2
                if u % 4 == 0 and hp >= 2:
                    pe.wait_ge(pv_evac, hp - 1)
                wait_aux_evac(pe, att_use(u, 1))
                o = banks[hp % 2][(h % 2) * DK:(h % 2 + 1) * DK, q * P:(q + 1) * P]
                nc.tensor.matmul(o, Vcm[:, g, :], PcT[:, R * q + r, :], start=True, stop=False)
                for b in range(2):
                    for t in range(q + 1):
                        mm = nc.tensor.matmul(o, vn[:, b, t, g * DK:(g + 1) * DK], pA[q][:, b * (q + 1) + t, :],
                                              start=False, stop=b == 1 and t == q)
                mm.then_inc(pv_done, 1)

            wait_aux_evac(pe, X["pct"] + 1)
            for u in range(34):
                if u < 32:
                    att_logits(u)
                if 1 <= u <= 32:
                    att_turn(u - 1)
                if u >= 2:
                    att_values(u - 2)
            pe.wait_ge(pv_evac, 8)
            with pe.Fori(0, 2) as i:
                for n in range(2):
                    rows_job(J_WOUT + n, A_WOUT + n, jd=i * 2, am=i * 2)
            pe.wait_ge(sk_landed, 16)
            for u in range(4):
                wait_aux_free(pe, X["skt"] + u)
                turn(X["skt"] + u, [(n * P, sk[:, 4 * u + n, :]) for n in range(4)])
            turn_stream(X["norm3"], 3)

            with pe.Fori(0, 2) as i:
                for n in range(2):
                    cols_job(J_WQ + n, A_WQ + n, jd=i * 2, am=i * 2)
                for n in range(2):
                    wait_acc_evac(pe, A_WQ + n, i * 2)
                    for m in range(MT):
                        k = X["psc"] + 2 * n + m
                        wait_aux_free(pe, k, i)
                        for f in range(4):
                            mm = nc.tensor.matmul(aux(k)[:, f * P:(f + 1) * P], qp[n][:, f, m * P:(m + 1) * P],
                                                  big[:, bass.ds(i * 1024 + (2048 + (4 * n + f) * P), P)],
                                                  start=True, stop=True)
                        mm.then_inc(aux_done, 1)

            pe.wait_ge(ple_landed, 32)
            wait_aux_free(pe, X["pt"])
            turn(X["pt"], [((2 * c + m) * P, pin[:, m, c * P:(c + 1) * P]) for c in range(2) for m in range(MT)])
            turn_stream(X["norm4"], 4)
            for n in range(NT):
                rows_job(J_GATE + n, A_GATE + n)
                for m in range(MT):
                    k = X["pp"] + 2 * n + m
                    wait_aux_free(pe, k)
                    for c in range(2):
                        mm = nc.tensor.matmul(aux(k)[:, :], pT[:, c, m * P:(m + 1) * P], plew[:, c, n * 512:n * 512 + 512],
                                              start=c == 0, stop=c == 1)
                    mm.then_inc(aux_done, 1)

        @block.gpsimd
        def _(pool):
            nc.gpsimd.memset(idxc[:, :], 0).then_inc(split_done, 8)
            pool.wait_ge(qk_norm, 2)
            nc.gpsimd.memset(flat[:, :, :, NCMP:], 0.0).then_inc(pads_ready, 1)
            wait_aux_evac(pool, X["qt"] + 3)
            nc.gpsimd.memset(big[:, 3584:3840], 0.0).then_inc(pads_ready, 1)
            pool.wait_ge(parts_used, used(J_WQ + 3))
            nc.gpsimd.memset(accx, 0.0).then_inc(acc_zero, 1)
            per = SLOTS // (GROUPS * EG)
            for g in range(GROUPS):
                pool.sem_inc(v_done[g], EG)

            def take_experts(m, i, g):
                nc.gpsimd.tensor_copy(idxc[:, g * EG:(g + 1) * EG],
                                      idx[:, bass.ds(i * (GROUPS * EG) + (m * SLOTS + g * EG), EG)]
                                      ).then_inc(idx_copied, 1)
                pool.wait_ge(idx_copied, 1)
                pool.sem_clear(idx_copied)

            def rows_u(g):
                for b in range(EG):
                    nc.gpsimd.indirect_dma_start(
                        out=ubuf[g][b], out_offset=None, in_=a["peer_u"],
                        in_offset=bass.IndirectOffsetOnAxis(ap=idxc[:, g * EG + b:g * EG + b + 1], axis=0),
                    ).then_inc(u_landed[g], 16)

            def rows_v(g):
                for b in range(EG):
                    nc.gpsimd.indirect_dma_start(
                        out=vbuf[g][b], out_offset=None, in_=a["peer_v"],
                        in_offset=bass.IndirectOffsetOnAxis(ap=idxc[:, g * EG + b:g * EG + b + 1], axis=0),
                    ).then_inc(v_landed[g], 16)

            pool.wait_ge(idx_ready, 1)
            for n in range(4):
                wait_aux_evac(pool, X["psc"] + 4 + n)
            for g in range(GROUPS):
                take_experts(0, 0, g)
                if g < 2:
                    rows_u(g)
                rows_v(g)
            pool.wait_ge(idx_ready, MT)
            pool.wait_ge(routed, MT)
            for g in range(2, GROUPS):
                rows_u(g)
            for m in range(MT):
                with pool.Fori(1 - m, per) as i:
                    for g in range(GROUPS):
                        pool.wait_ge(v_done[g], EG * m * per + EG + i * EG)
                        take_experts(m, i, g)
                        rows_u(g)
                        rows_v(g)


_SQUEEZE = {"x": "x", "sb_w_qkv": "sb_w_qkv", "sb_w_o": "sb_w_o", "norm_mix": "norm_mix", "norm_mlp": "norm_mlp",
            "mlp_w1": "mlp_w1", "mlp_w2": "mlp_w2", "p": "p_2", "mix_norm_w": "mix_norm_w_2", "w_in": "w_in_2",
            "q_norm_w": "q_norm_w_2", "k_norm_w": "k_norm_w_2", "cmp_k_pos": "cmp_k_pos_2", "cmp_k_w1": "cmp_k_w1_2",
            "cmp_k_b1": "cmp_k_b1_2", "cmp_k_w2": "cmp_k_w2_2", "cmp_v_pos": "cmp_v_pos_2", "cmp_v_w1": "cmp_v_w1_2",
            "cmp_v_b1": "cmp_v_b1_2", "cmp_v_w2": "cmp_v_w2_2", "pool_w": "pool_w_2", "pool_scale": "pool_scale_2",
            "w_out": "w_out_2", "ffn_norm_w": "ffn_norm_w_2", "peer_w_q": "peer_w_q_2",
            "peer_sub_keys": "peer_sub_keys_2", "peer_u": "peer_u_2", "peer_v": "peer_v_2",
            "ple_norm_w": "ple_norm_w_2", "ple_w_gate": "ple_w_gate_2", "ple_w_proj": "ple_w_proj_2"}
_WHOLE = {"final_norm": "final_norm", "rel_bias": "rel_bias_2"}


def kernel(**inputs):
    import concourse.bacc as bacc
    from concourse.bass_utils import run_bass_kernel_spmd

    nc = bacc.Bacc("TRN2", target_bir_lowering=False, num_devices=1)
    arrays, aps = {}, {}

    def give(name, x):
        x = np.ascontiguousarray(x)
        arrays[f"in_{name}"] = x
        aps[name] = nc.dram_tensor(f"in_{name}", x.shape, mybir.dt.from_np(x.dtype), kind="ExternalInput").ap()

    for name, given in _SQUEEZE.items():
        x = np.asarray(inputs[given])
        give(name, x.reshape(x.shape[2:] if name == "p" else x.shape[1:]))
    for name, given in _WHOLE.items():
        give(name, inputs[given])
    for name, x in host_constants().items():
        give(name, x)
    out = nc.dram_tensor("out", (S, D), F32, kind="ExternalOutput").ap()
    line_dram = nc.dram_tensor("line", (16, 512), F32, kind="Internal").ap()
    build(nc, aps, out, line_dram)
    r = run_bass_kernel_spmd(nc, [arrays], core_ids=[0])
    return r.results[0]["out"].reshape(1, S, D)
```
